# Optimizing a Trainium2 kernel written in Bass

```python
import math
import jax
import jax.numpy as jnp
from jax import lax
import numpy as np

D_MODEL = 2048
BATCH = 1
SEQ = 256
DEPTH = 1

GLA_HEADS = 4
GLA_DK = 256
GLA_DV = 512
GLA_GATE_RANK = 16
GLA_GATE_TEMP = 16.0
GLA_CHUNK = 64
DSA_HEADS = 16
DSA_HEAD_DIM = 128
IDX_HEADS = 16
IDX_DIM = 64
DSA_TOPK = 256
DSA_QBLOCK = 128
MEM_LEN = 256
XATTN_HEADS = 4
XATTN_HEAD_DIM = D_MODEL // XATTN_HEADS
PEER_HEADS = 8
PEER_NKEYS = 128
PEER_NEXPERTS = PEER_NKEYS * PEER_NKEYS
PEER_KEY_DIM = 256
PEER_HALF = PEER_KEY_DIM // 2
PEER_TOPK = 16
PEER_BLOCK = 64
ROPE_THETA = 10000.0
RMS_EPS = 1e-6

IN_WIDTHS = (
    GLA_HEADS * GLA_DK,
    GLA_HEADS * GLA_DK,
    GLA_HEADS * GLA_DV,
    GLA_HEADS * GLA_DV,
    GLA_GATE_RANK,
    DSA_HEADS * DSA_HEAD_DIM,
    DSA_HEAD_DIM,
    DSA_HEAD_DIM,
    IDX_HEADS * IDX_DIM,
    IDX_DIM,
    IDX_HEADS,
    D_MODEL,
    D_MODEL,
)
IN_DIM = sum(IN_WIDTHS)

kernel_name = "hybrid_gla_dsa_peer_block"

def rms_norm(x, g):
    xf = x.astype(jnp.float32)
    y = xf * lax.rsqrt(jnp.mean(xf * xf, axis=-1, keepdims=True) + RMS_EPS)
    return (y * g.astype(jnp.float32)).astype(x.dtype)

def rope(x, pos):
    d = x.shape[-1]
    inv = ROPE_THETA ** (-jnp.arange(0, d, 2, dtype=jnp.float32) / d)
    ang = pos.astype(jnp.float32)[..., None] * inv
    cos = jnp.cos(ang)[:, :, None, :]
    sin = jnp.sin(ang)[:, :, None, :]
    xf = x.astype(jnp.float32)
    x1, x2 = xf[..., : d // 2], xf[..., d // 2:]
    out = jnp.concatenate([x1 * cos - x2 * sin, x2 * cos + x1 * sin], axis=-1)
    return out.astype(x.dtype)

def split_cols(p):
    points, acc = [], 0
    for w in IN_WIDTHS[:-1]:
        acc += w
        points.append(acc)
    return jnp.split(p, points, axis=-1)

def gla_chunked(q, k, v, log_a):
    B, S, H, dk = q.shape
    dv = v.shape[-1]
    C = GLA_CHUNK
    nc = S // C

    def to_chunks(t):
        return t.astype(jnp.float32).reshape(B, nc, C, H, -1).transpose(1, 0, 3, 2, 4)

    qc = to_chunks(q * (dk ** -0.5))
    kc, vc, gc = to_chunks(k), to_chunks(v), to_chunks(log_a)
    causal = jnp.tril(jnp.ones((C, C), dtype=bool))[None, None, :, :, None]

    def step(state, inp):
        qb, kb, vb, gb = inp
        b = jnp.cumsum(gb, axis=2)
        o_inter = jnp.einsum('bhcd,bhde->bhce', qb * jnp.exp(b), state)
        diff = jnp.where(causal, b[:, :, :, None, :] - b[:, :, None, :, :], -jnp.inf)
        attn = jnp.einsum('bhijd,bhjd->bhij', qb[:, :, :, None, :] * jnp.exp(diff), kb)
        o_intra = jnp.einsum('bhij,bhje->bhie', attn, vb)
        b_last = b[:, :, -1:, :]
        new_state = jnp.exp(b_last[:, :, 0, :])[..., None] * state + jnp.einsum(
            'bhjd,bhje->bhde', kb * jnp.exp(b_last - b), vb)
        return new_state, o_inter + o_intra

    s0 = jnp.zeros((B, H, dk, dv), jnp.float32)
    _, o = lax.scan(step, s0, (qc, kc, vc, gc))
    return o.transpose(1, 0, 3, 2, 4).reshape(B, S, H, dv).astype(q.dtype)

def dsa_attention(q, k, v, q_idx, k_idx, w_idx):
    B, S, H, dh = q.shape
    topk = min(DSA_TOPK, S // 4)
    QB = DSA_QBLOCK
    nblk = S // QB
    key_pos = jnp.arange(S)
    scale = dh ** -0.5

    def block(i):
        t0 = i * QB
        q_b = lax.dynamic_slice_in_dim(q, t0, QB, axis=1)
        qi_b = lax.dynamic_slice_in_dim(q_idx, t0, QB, axis=1)
        w_b = lax.dynamic_slice_in_dim(w_idx, t0, QB, axis=1)
        t_pos = t0 + jnp.arange(QB)
        s_idx = jnp.einsum('bqhd,bsd->bqhs', qi_b, k_idx).astype(jnp.float32) * (IDX_DIM ** -0.5)
        score = jnp.einsum('bqhs,bqh->bqs', jax.nn.relu(s_idx),
                           w_b.astype(jnp.float32)) * (IDX_HEADS ** -0.5)
        visible = key_pos[None, :] <= t_pos[:, None]
        score = jnp.where(visible[None], score, -jnp.inf)
        _, sel = lax.top_k(score, topk)
        k_sel = jax.vmap(lambda kk, ii: kk[ii])(k, sel)
        v_sel = jax.vmap(lambda vv, ii: vv[ii])(v, sel)
        valid = sel <= t_pos[None, :, None]
        logits = jnp.einsum('bqhd,bqkd->bhqk', q_b, k_sel).astype(jnp.float32) * scale
        logits = jnp.where(valid[:, None], logits, -jnp.inf)
        p = jax.nn.softmax(logits, axis=-1).astype(v.dtype)
        return jnp.einsum('bhqk,bqkd->bqhd', p, v_sel)

    out = lax.map(block, jnp.arange(nblk))
    return out.transpose(1, 0, 2, 3, 4).reshape(B, S, H, dh)

def memory_cross_attention(hn, memn, wq, wk, wv, wo):
    B, S, _ = hn.shape
    M = memn.shape[1]
    q = (hn @ wq).reshape(B, S, XATTN_HEADS, XATTN_HEAD_DIM)
    k = (memn @ wk).reshape(B, M, XATTN_HEADS, XATTN_HEAD_DIM)
    v = (memn @ wv).reshape(B, M, XATTN_HEADS, XATTN_HEAD_DIM)
    logits = jnp.einsum('bshd,bmhd->bhsm', q, k).astype(jnp.float32) * (XATTN_HEAD_DIM ** -0.5)
    p = jax.nn.softmax(logits, axis=-1).astype(v.dtype)
    o = jnp.einsum('bhsm,bmhd->bshd', p, v).reshape(B, S, XATTN_HEADS * XATTN_HEAD_DIM)
    return o @ wo

def peer_ffn(xn, wq, sub_keys, u_tab, v_tab):
    B, S, D = xn.shape
    q = (xn @ wq).reshape(B, S, PEER_HEADS, 2, PEER_HALF)
    s = jnp.einsum('bshpd,hpnd->bshpn', q, sub_keys).astype(jnp.float32)
    top_v, top_i = lax.top_k(s, PEER_TOPK)
    cand = (top_v[..., 0, :, None] + top_v[..., 1, None, :]).reshape(B, S, PEER_HEADS, PEER_TOPK * PEER_TOPK)
    cand_v, cand_i = lax.top_k(cand, PEER_TOPK)
    i1 = jnp.take_along_axis(top_i[..., 0, :], cand_i // PEER_TOPK, axis=-1)
    i2 = jnp.take_along_axis(top_i[..., 1, :], cand_i % PEER_TOPK, axis=-1)
    experts = i1 * PEER_NKEYS + i2
    gates = jax.nn.softmax(cand_v, axis=-1).astype(xn.dtype)
    T = B * S
    nb = T // PEER_BLOCK
    x_b = xn.reshape(nb, PEER_BLOCK, D)
    e_b = experts.reshape(nb, PEER_BLOCK, PEER_HEADS * PEER_TOPK)
    g_b = gates.reshape(nb, PEER_BLOCK, PEER_HEADS * PEER_TOPK)

    def block(args):
        xb, eb, gb = args
        act = jax.nn.gelu(jnp.einsum('td,tkd->tk', xb, u_tab[eb]))
        return jnp.einsum('tk,tkd->td', gb * act, v_tab[eb])

    out = lax.map(block, (x_b, e_b, g_b))
    return out.reshape(B, S, D)

def setup_inputs(seed: int = 0) -> dict:
    key = jax.random.key(seed)
    ks = jax.random.split(key, 24)
    f32 = jnp.float32
    D = D_MODEL
    L = DEPTH

    def nrm(k, shape, scale):
        return jax.random.normal(k, shape, f32) * scale

    def gain(k, shape):
        return 1.0 + 0.02 * jax.random.normal(k, shape, f32)

    return {
        "x": nrm(ks[0], (BATCH, SEQ, D), 1.0),
        "mem": nrm(ks[1], (BATCH, MEM_LEN, D), 1.0),
        "positions": jnp.broadcast_to(jnp.arange(SEQ, dtype=jnp.int32), (BATCH, SEQ)),
        "norm_mix_g": gain(ks[2], (L, D)),
        "w_in": nrm(ks[3], (L, D, IN_DIM), D ** -0.5),
        "gla_gate_w2": nrm(ks[4], (L, GLA_GATE_RANK, GLA_HEADS * GLA_DK), GLA_GATE_RANK ** -0.5),
        "gla_gate_b": nrm(ks[5], (L, GLA_HEADS * GLA_DK), 0.1),
        "gla_head_norm_g": gain(ks[6], (L, GLA_HEADS, GLA_DV)),
        "w_proj_gla": nrm(ks[7], (L, GLA_HEADS * GLA_DV, D), (GLA_HEADS * GLA_DV) ** -0.5),
        "w_proj_dsa": nrm(ks[8], (L, DSA_HEADS * DSA_HEAD_DIM, D), (DSA_HEADS * DSA_HEAD_DIM) ** -0.5),
        "w_out": nrm(ks[9], (L, D, D), D ** -0.5),
        "norm_x_g": gain(ks[10], (L, D)),
        "norm_mem_g": gain(ks[11], (L, D)),
        "w_xq": nrm(ks[12], (L, D, XATTN_HEADS * XATTN_HEAD_DIM), D ** -0.5),
        "w_xk": nrm(ks[13], (L, D, XATTN_HEADS * XATTN_HEAD_DIM), D ** -0.5),
        "w_xv": nrm(ks[14], (L, D, XATTN_HEADS * XATTN_HEAD_DIM), D ** -0.5),
        "w_xo": nrm(ks[15], (L, XATTN_HEADS * XATTN_HEAD_DIM, D), (XATTN_HEADS * XATTN_HEAD_DIM) ** -0.5),
        "norm_ffn_g": gain(ks[16], (L, D)),
        "peer_wq": nrm(ks[17], (L, D, PEER_HEADS * PEER_KEY_DIM), D ** -0.5),
        "peer_sub_keys": nrm(ks[18], (L, PEER_HEADS, 2, PEER_NKEYS, PEER_HALF), PEER_HALF ** -0.5),
        "peer_u": nrm(ks[19], (L, PEER_NEXPERTS, D), D ** -0.5),
        "peer_v": nrm(ks[20], (L, PEER_NEXPERTS, D), 0.5),
        "norm_final_g": gain(ks[21], (D,)),
    }

def reference(x, mem, positions, norm_mix_g, w_in, gla_gate_w2, gla_gate_b, gla_head_norm_g,
              w_proj_gla, w_proj_dsa, w_out, norm_x_g, norm_mem_g, w_xq, w_xk, w_xv, w_xo,
              norm_ffn_g, peer_wq, peer_sub_keys, peer_u, peer_v, norm_final_g):
    B, S, D = x.shape
    h = x
    for l in range(DEPTH):
        a = rms_norm(h, norm_mix_g[l])
        (g_q, g_k, g_v, g_r, g_low, d_q, d_k, d_v, i_q, i_k, i_w, gate_a, gate_b) = split_cols(a @ w_in[l])

        log_a = jax.nn.log_sigmoid((g_low @ gla_gate_w2[l] + gla_gate_b[l]).astype(jnp.float32)) / GLA_GATE_TEMP
        o_a = gla_chunked(g_q.reshape(B, S, GLA_HEADS, GLA_DK),
                          g_k.reshape(B, S, GLA_HEADS, GLA_DK),
                          g_v.reshape(B, S, GLA_HEADS, GLA_DV),
                          log_a.reshape(B, S, GLA_HEADS, GLA_DK))
        o_a = rms_norm(o_a, gla_head_norm_g[l]).reshape(B, S, GLA_HEADS * GLA_DV) * jax.nn.silu(g_r)
        y_a = o_a @ w_proj_gla[l]

        q_b = rope(d_q.reshape(B, S, DSA_HEADS, DSA_HEAD_DIM), positions)
        k_b = rope(d_k[:, :, None, :], positions)[:, :, 0, :]
        qi = rope(i_q.reshape(B, S, IDX_HEADS, IDX_DIM), positions)
        ki = rope(i_k[:, :, None, :], positions)[:, :, 0, :]
        o_b = dsa_attention(q_b, k_b, d_v, qi, ki, i_w).reshape(B, S, DSA_HEADS * DSA_HEAD_DIM)
        y_b = o_b @ w_proj_dsa[l]

        merged = jax.nn.sigmoid(gate_a) * y_a + jax.nn.sigmoid(gate_b) * y_b
        h = h + merged @ w_out[l]

        h = h + memory_cross_attention(rms_norm(h, norm_x_g[l]), rms_norm(mem, norm_mem_g[l]),
                                       w_xq[l], w_xk[l], w_xv[l], w_xo[l])

        h = h + peer_ffn(rms_norm(h, norm_ffn_g[l]), peer_wq[l], peer_sub_keys[l], peer_u[l], peer_v[l])
    return rms_norm(h, norm_final_g)


_drawn_inputs = setup_inputs


def setup_inputs(seed=0):
    import zlib

    import numpy as np

    out = dict(_drawn_inputs(seed))
    spreads = {}
    factors = {'gla_head_norm_g': 2.787,
     'norm_x_g': 4.819,
     'norm_mem_g': 3.886,
     'norm_final_g': 7.622,
     'norm_ffn_g': 5.867}
    for name, (base, spread) in spreads.items():
        noise = np.random.default_rng([zlib.crc32(name.encode()), seed]).standard_normal(out[name].shape)
        drawn = base * np.exp(spread * noise) if base else spread * noise
        out[name] = jnp.asarray(drawn.astype(out[name].dtype))
    for name, factor in factors.items():
        out[name] = (out[name] * factor).astype(out[name].dtype)
    return out
```

```python
from contextlib import ExitStack, contextmanager

import numpy as np

import concourse.bass as bass
from concourse import mybir

F32 = mybir.dt.float32
F32R = mybir.dt.float32r
I32 = mybir.dt.int32
U32 = mybir.dt.uint32
ALU = mybir.AluOpType
ACT = mybir.ActivationFunctionType
AX = mybir.AxisListType

P = 128
T = 256
TT = T // P
D = 2048
KT = D // P
CH = 256
UQ = 4
UK = KT // UQ
EPS = 1e-6

GLA_H, DK, DV, RANK = 4, 256, 512, 16
GATE_TEMP = 16.0
DSA_H, DH, IDX_H, IDX_D = 16, 128, 16, 64
TOPK = min(256, T // 4)
XH, XD = 4, D // 4
PEER_H, NKEYS, PTOP = 8, 128, 16
GROUPS = TT * PEER_H
RING = 8

COL = {}
_at = 0
for _name, _w in (("g_q", GLA_H * DK), ("g_k", GLA_H * DK), ("g_v", GLA_H * DV), ("g_r", GLA_H * DV), ("g_low", RANK),
                  ("d_q", DSA_H * DH), ("d_k", DH), ("d_v", DH), ("i_q", IDX_H * IDX_D), ("i_k", IDX_D), ("i_w", IDX_H),
                  ("gate_a", D), ("gate_b", D)):
    COL[_name] = _at
    _at += _w
IN_DIM = _at

IQ = 0
DQ = IQ + 2
GB = DQ + 4
GL = GB + 8
GA = GL + 12
XK = GA + 8
WO = XK + 4
XV = WO + 4
XQ = XV + 4
XO = XQ + 4
PQ = XO + 4
END = PQ + 4

LEVELS = (64, 32, 16, 8, 4, 2, 1)
C_IDENT = 0
C_MASK = P
C_COLS = C_MASK + P * len(LEVELS)
C_IOTA = C_COLS + 8
C_END = C_IOTA + PTOP
INV_D, SGN_D, INV_I, SGN_I, EPSC = range(C_COLS, C_COLS + 5)

G_MIX, G_X, G_MEM, G_FFN, G_HEAD, G_BIAS, G_ROWS = 0, 16, 32, 48, 64, 80, 88

TWO_PI_1 = 6.28125
TWO_PI_2 = 0.00193500518798828125
TWO_PI_3 = 2 * np.pi - TWO_PI_1 - TWO_PI_2
ROUND = 1.5 * 2.0 ** 23
PI = 3.1415925
HIDDEN = -1.0e38
TAKEN = -3.0e38
NEG = -1.0e30


def constants():
    c = np.zeros((P, C_END), np.float32)
    c[:, C_IDENT:C_IDENT + P] = np.eye(P, dtype=np.float32)
    j, i = np.arange(P)[:, None], np.arange(P)[None, :]
    for n, m in enumerate(LEVELS):
        c[:, C_MASK + n * P:C_MASK + (n + 1) * P] = (j // (2 * m) == i // (2 * m)) & (j % (2 * m) < m) & (i % (2 * m) >= m)
    for d, inv, sgn in ((DH, INV_D, SGN_D), (IDX_D, INV_I, SGN_I)):
        freq = np.float32(10000.0) ** (-np.arange(0, d, 2, dtype=np.float32) / np.float32(d))
        k = np.arange(P) % d
        c[:, inv] = freq[k % (d // 2)]
        c[:, sgn] = np.where(k < d // 2, -1.0, 1.0)
    c[:, EPSC] = EPS
    c[:, C_IOTA:] = np.arange(PTOP, dtype=np.float32)
    return c


class Chain:

    def __init__(self, eng, sem, apart):
        self.eng, self.sem, self.apart, self.base, self.n = eng, sem, apart, 0, 0

    def __call__(self, ins):
        ins.then_inc(self.sem, 1)
        self.n += 1
        self.apart(self.sem, self.base + self.n)

    @contextmanager
    def loop(self, lo, hi, per):
        start = self.base + self.n
        with self.eng.Fori(lo, hi) as i:
            self.base, self.n = i * per + (start - lo * per), 0
            yield i
            assert self.n == per, f"the body has {self.n} chained steps, not {per}"
        self.base, self.n = start + (hi - lo) * per, 0


class Apart:

    def __init__(self, eng, met):
        self.eng, self.met, self.value = eng, met, eng.alloc_register("wait_value")

    def __call__(self, sem, value):
        if isinstance(value, int):
            wait(self.eng, sem, value)
        else:
            self.eng.reg_mov(self.value, value)
            self.eng.wait_ge(self.met, 1)
            self.eng.wait_ge(sem, self.value)


def wait(eng, sem, value):
    if not isinstance(value, int) or value > 0:
        eng.wait_ge(sem, value)


def hybrid_block(nc, a):
    ctx = ExitStack()
    sems = {}

    def sem(name):
        if name not in sems:
            sems[name] = ctx.enter_context(nc.semaphore(name))
        return sems[name]

    base = (nc.sbuf_base + 63) // 64 * 64
    K = 1024

    def sb(name, shape, at, dt=F32):
        return nc.alloc_sbuf_tensor_at("b_" + name, [P] + list(shape), dt, offset=base + int(at))[:]

    RAW, HI, LO, ACTV, ATTN, HT, SCR, MRG, WRK, SML = (0, 32 * K, 48 * K, 64 * K, 96 * K, 128 * K, 144 * K, 160 * K,
                                                       176 * K, 192 * K)
    raw = sb("raw", [2 * UQ, UK, CH], RAW)
    w_hi = sb("w_hi", [UQ, UK, CH], HI, F32R)
    w_lo = sb("w_lo", [UQ, UK, CH], LO, F32R)
    act_hi = sb("act_hi", [KT, T], ACTV, F32R)
    act_lo = sb("act_lo", [KT, T], ACTV + 16 * K, F32R)
    att_hi = sb("att_hi", [KT, T], ATTN, F32R)
    att_lo = sb("att_lo", [KT, T], ATTN + 16 * K, F32R)
    hT = sb("hT", [KT, T], HT)
    scr = sb("scr", [KT, T], SCR)
    merged = sb("merged", [KT, T], MRG)
    xN = sb("xN", [TT, D], MRG)
    kcT = sb("kcT", [KT, T], MRG)
    vcN = sb("vcN", [TT, D], WRK)
    memN = sb("memN", [TT, D], SCR)
    memT = sb("memT", [KT, T], WRK)
    SMALLW = 3 * P + IDX_H + RANK
    small_w = sb("small_w", [KT, SMALLW], ATTN)
    cos_d, sin_d, cos_i, sin_i = (sb(n, [T], WRK + k * K) for k, n in enumerate(("cos_d", "sin_d", "cos_i", "sin_i")))
    kiT = sb("kiT", [T], WRK + 4 * K)
    kdT = sb("kdT", [T], WRK + 5 * K)
    vdN = sb("vdN", [TT, DH], WRK + 6 * K)
    score = sb("score", [3 * P], WRK + 7 * K)
    sel_work = sb("sel_work", [3 * P], WRK + 8.5 * K)
    keep = sb("keep", [3 * P], WRK + 10 * K)
    relu = sb("relu", [2, 3 * P], WRK + 11.5 * K)
    idx_w = sb("idx_w", [TT, IDX_H], WRK + 14.5 * K)
    top8 = sb("top8", [8], WRK + 14.75 * K)
    pos_i = sb("pos_i", [T], WRK + 7 * K, I32)
    pos_f = sb("pos_f", [T], WRK + 8 * K)
    angle = sb("angle", [T], WRK + 9 * K)
    turns = sb("turns", [T], WRK + 10 * K)
    qbuf = sb("qbuf", [2, 2, T], SCR)
    swap = sb("swap", [2, T], SCR + 4 * K)
    rot = sb("rot", [2, T], SCR + 6 * K)
    probs = sb("probs", [4, 3, P], SCR + 8 * K)
    cum = sb("cum", [2 * GLA_H, T], WRK)
    attn = sb("attn", [3, P], WRK + 8 * K)
    decay = [sb(f"decay{n}", [2, T], WRK + (9.5 + 2 * n) * K) for n in range(2)]
    osq = sb("osq", [4, T], WRK + 9.5 * K)
    gz = sb("gz", [8, T], SCR)
    ge = sb("ge", [8, T], SCR + 8 * K)
    qg = sb("qg", [2, T], SCR)
    kg = sb("kg", [2, T], SCR + 2 * K)
    onorm = sb("onorm", [4, T], SCR)
    vg = sb("vg", [TT, DV], SCR + 4 * K)
    swish = sb("swish", [4, T], SCR + 8 * K)
    zlev = [sb("zlev0", [2, T], SCR + 12 * K), sb("zlev1", [2, T], SCR + 14 * K), sb("zlev2", [2, T], WRK + 13.5 * K)]
    qx = sb("qx", [4, T], SCR)
    px = sb("px", [TT, T], SCR + 4 * K)
    pxT = sb("pxT", [TT, T], SCR + 6 * K)
    hN = sb("hN", [TT, D], WRK)
    xnN = sb("xnN", [TT, D], HT)
    skN = sb("skN", [2 * PEER_H, P], MRG)
    skT = sb("skT", [2 * PEER_H, P], MRG + 8 * K)
    qp = sb("qp", [2, 2, T], MRG)
    sims = sb("sims", [GROUPS, 2, NKEYS], SCR)
    gfin = sb("gfin", [D], MRG)
    R = MRG + 8 * K
    sc = sb("sc", [2, NKEYS], R)
    sc2 = sb("sc2", [2, NKEYS], R + K)
    cand = sb("cand", [PTOP, PTOP], R + 2 * K)
    cand2 = sb("cand2", [PTOP, PTOP], R + 3 * K)
    onehot = sb("onehot", [PTOP, PTOP], R + 4 * K)
    idx_all = sb("idx_all", [GROUPS * PTOP], R + 5 * K, U32)
    gates_all = sb("gates_all", [GROUPS * PTOP], R + 6 * K)
    s0 = R + 7 * K
    tv = sb("tv", [2, PTOP], s0)
    ti = sb("ti", [2, PTOP], s0 + 128, U32)
    tif = sb("tif", [2, PTOP], s0 + 256)
    cv = sb("cv", [PTOP], s0 + 384)
    ci = sb("ci", [PTOP], s0 + 448, U32)
    cpart = sb("cpart", [2, PTOP], s0 + 512, U32)
    cpartf = sb("cpartf", [2, PTOP], s0 + 640)
    isel = sb("isel", [2, PTOP], s0 + 768)
    urow = sb("urow", [RING, D], RAW)
    vrow = sb("vrow", [RING, D], ACTV)
    consts = sb("consts", [C_END], SML)
    s1 = SML + 4 * ((C_END + 7) // 8 * 8)
    ones = sb("ones", [T], s1)
    gains = sb("gains", [G_ROWS], s1 + K)
    g_low = sb("g_low", [T], s1 + K + 384)
    rstd = sb("rstd", [T], s1 + 2 * K + 384)
    masked = sb("masked", [TT, P], s1 + 3 * K + 384)
    sg = sb("sg", [2, 2, T], s1 + 4 * K + 384)
    gain_rows = sb("gain_rows", [P], s1 + 4 * K + 384)
    w2 = sb("w2", [GLA_H * DK], s1 + 4 * K + 384)
    diag = sb("diag", [4, P], s1 + 4 * K + 384)
    s2 = s1 + 8 * K + 384
    negmax = sb("negmax", [8], s2)
    psums = sb("psums", [8], s2 + 32)
    prec = sb("prec", [8], s2 + 64)
    gsum = sb("gsum", [8], s2 + 96)
    stat = sb("stat", [8], s2 + 128)
    egate = sb("egate", [PTOP], s2 + 160)
    dots = sb("dots", [PTOP], s2 + 224)
    gelu = sb("gelu", [PTOP], s2 + 288)
    wexp = sb("wexp", [PTOP], s2 + 352)
    stage_idx = sb("stage_idx", [4, PTOP], s2 + 416, U32)
    assert base + s2 + 672 <= nc.sbuf_usable_end

    ident = consts[:, C_IDENT:C_IDENT + P]

    def const(n):
        return consts[:, n:n + 1]

    def mask(n):
        return consts[:, C_MASK + n * P:C_MASK + (n + 1) * P]

    bank = [nc.alloc_psum_tensor(f"bank{n}", [P, 512], F32)[:] for n in range(8)]
    proj = [bank[c].rearrange("p (n t) -> p n t", n=2) for c in range(2)]

    w_landed = [sem(f"w_landed{s}") for s in range(2 * UQ)]
    w_high = sem("w_high")
    w_split = sem("w_split")
    units_used = sem("units_used")
    bank_free = [sem(f"bank_free{c}") for c in range(2)]

    def unit(p, c, q=0):
        return 8 * p + 4 * c + q

    def halves(x, m):
        return x.rearrange("p a (n s m) -> p (a n) s m", s=2, m=m)

    def load_pair(sp, apart, p, sources):
        for c, (w, col) in enumerate(sources):
            rows = w.rearrange("(q k p) n -> q p k n", q=UQ, p=P)
            for q in range(UQ):
                apart(w_split, unit(p, c, q) - 2 * UQ + 1)
                sp.dma_start(raw[:, UQ * c + q], rows[q][:, :, bass.ds(col, CH)]).then_inc(w_landed[UQ * c + q], 16)

    def split_high(act, p, c):
        for q in range(UQ):
            act.wait_ge(w_landed[UQ * c + q], p * 16 + 16)
            wait(act, units_used, unit(p, c, q) - UQ + 1)
            act.activation(w_hi[:, q], raw[:, UQ * c + q], ACT.Copy).then_inc(w_high, 1)

    def split_low(dve, p, c):
        for q in range(UQ):
            dve.wait_ge(w_high, unit(p, c, q) + 1)
            dve.tensor_tensor(w_lo[:, q], raw[:, UQ * c + q], w_hi[:, q].bitcast(F32), ALU.subtract).then_inc(w_split, 1)

    def multiply(pe, p, c, hi, lo, tokens_out=False):
        wait(pe, bank_free[c], p)
        for q in range(UQ):
            pe.wait_ge(w_split, unit(p, c, q) + 1)
            for n in range(2):
                for k in range(UK):
                    kt = UK * q + k
                    for t, (x, w) in enumerate(((hi, w_hi), (lo, w_hi), (hi, w_lo))):
                        if tokens_out:
                            lhs, rhs = x[:, kt, n * P:(n + 1) * P], w[:, q, k, :]
                        else:
                            lhs, rhs = w[:, q, k, n * P:(n + 1) * P], x[:, kt, :]
                        mm = pe.matmul(proj[c][:, n], lhs, rhs, start=(q == 0 and n == 0 and k == 0 and t == 0),
                                       stop=(q == UQ - 1 and k == UK - 1 and t == 2), skip_group_check=True)
            mm.then_inc(units_used, 1)

    def multiplied(eng, p, c):
        eng.wait_ge(units_used, unit(p, c + 1))

    def evacuating(eng, split, p, evac, last=False):
        split(eng, p, 1)
        evac(p, 0)
        if not last:
            split(eng, p + 1, 0)
        evac(p, 1)

    def nothing(p, c):
        pass

    def norm_squares(act, tag, src, turned=None):
        for q in range(4):
            if turned is not None:
                act.wait_ge(turned, 2 * q + 2)
            act.activation(scr[:, 4 * q:4 * q + 4], src[:, 4 * q:4 * q + 4], ACT.Square).then_inc(sem(tag + "_squares"), 1)

    def norm_sums(pe, tag):
        for q in range(4):
            pe.wait_ge(sem(tag + "_squares"), q + 1)
            for k in range(4 * q, 4 * q + 4):
                mm = pe.matmul(bank[6][:, 0:T], ones[:, 0:P], scr[:, k], start=(k == 0), stop=(k == KT - 1))
        mm.then_inc(sem(tag + "_sums"), 1)

    def norm_root(act, tag):
        act.wait_ge(sem(tag + "_sums"), 1)
        act.activation(rstd, bank[6][:, 0:T], ACT.Sqrt, scale=1.0 / D, bias=const(EPSC)).then_inc(sem(tag + "_root"), 1)

    def norm_scale(dve, link, tag, src, row):
        dve.wait_ge(sem(tag + "_root"), 1)
        link(dve.reciprocal(rstd, rstd))
        for k in range(KT):
            ins = dve.scalar_tensor_tensor(out=scr[:, k], in0=src[:, k], scalar=gains[:, row + k:row + k + 1], in1=rstd,
                                           op0=ALU.mult, op1=ALU.mult)
            if k % 4 == 3:
                ins.then_inc(sem(tag + "_scaled"), 1)

    def operand_high(act, ready, tag, src, hi):
        for q in range(4):
            if ready is not None:
                act.wait_ge(ready, q + 1)
            act.activation(hi[:, 4 * q:4 * q + 4], src[:, 4 * q:4 * q + 4], ACT.Copy).then_inc(sem(tag + "_high"), 1)

    def operand_low(dve, tag, src, hi, lo):
        for q in range(4):
            dve.wait_ge(sem(tag + "_high"), q + 1)
            s = slice(4 * q, 4 * q + 4)
            dve.tensor_tensor(lo[:, s], src[:, s], hi[:, s].bitcast(F32), ALU.subtract).then_inc(sem(tag + "_operand"), 1)

    def turn_in(pe, tag, src):
        for j in range(8):
            if j >= 4:
                pe.wait_ge(sem(tag + "_copied"), j - 3)
            for k in range(2):
                for t in range(TT):
                    mm = pe.transpose(bank[2 + j % 4][:, k * T + t * P:k * T + (t + 1) * P],
                                      src[:, t, (2 * j + k) * P:(2 * j + k + 1) * P], ident)
            mm.then_inc(sem(tag + "_turned"), 1)

    def copy_in(act, tag, dst):
        for j in range(8):
            act.wait_ge(sem(tag + "_turned"), j + 1)
            act.activation(dst[:, 2 * j:2 * j + 2], bank[2 + j % 4].rearrange("p (k t) -> p k t", k=2),
                           ACT.Copy).then_inc(sem(tag + "_copied"), 1)

    u_landed = [sem(f"u_landed{s}") for s in range(RING)]
    v_landed = [sem(f"v_landed{s}") for s in range(RING)]
    w_in = a["w_in"][0]

    def square(name):
        return a[name][0]

    block = ctx.enter_context(nc.Block())

    @block.sync
    def _(sp):
        apart = Apart(sp, w_split)
        sp.dma_start(xN, a["x"][0].rearrange("(t p) d -> p t d", p=P)).then_inc(sem("x_landed"), 16)
        for i in range(2):
            load_pair(sp, apart, IQ + i, [(w_in, COL["i_q"] + (2 * i + c) * CH) for c in range(2)])

        def stream(first, lo, hi, w, col=0):
            with sp.Fori(lo, hi) as i:
                load_pair(sp, apart, first + i, [(w, i * 2 * CH + col + c * CH) for c in range(2)])

        def gated(first, gate, w):
            with sp.Fori(0, 4) as i:
                load_pair(sp, apart, i * 2 + first, [(w_in, i * 2 * CH + COL[gate] + c * CH) for c in range(2)])
                load_pair(sp, apart, i * 2 + first + 1, [(w, i * 2 * CH + c * CH) for c in range(2)])

        stream(DQ, 0, 4, w_in, COL["d_q"])
        gated(GB, "gate_b", square("w_proj_dsa"))
        with sp.Fori(0, GLA_H) as h:
            load_pair(sp, apart, h * 3 + GL, [(w_in, h * DK + COL[n]) for n in ("g_q", "g_k")])
            load_pair(sp, apart, h * 3 + GL + 1, [(w_in, h * DV + COL["g_v"] + c * CH) for c in range(2)])
            load_pair(sp, apart, h * 3 + GL + 2, [(w_in, h * DV + COL["g_r"] + c * CH) for c in range(2)])
        gated(GA, "gate_a", square("w_proj_gla"))
        for first, name in ((XK, "w_xk"), (WO, "w_out"), (XV, "w_xv"), (XQ, "w_xq"), (XO, "w_xo"), (PQ, "peer_wq")):
            stream(first, 0, 4, square(name))
        for t in range(TT):
            sp.wait_ge(sem("out_ready"), t + 1)
            sp.dma_start(a["out"][0, t * P:(t + 1) * P], hN[:, t]).then_inc(sem("out_stored"), 16)
        sp.wait_ge(sem("out_stored"), 16 * TT)

    @block.gpsimd
    def _(pool):
        apart = Apart(pool, sem("keep_ready"))

        def drop_hidden(out, in_, fill, done):
            pool.affine_select(out=out[:, 0:P], in_=in_[:, 0:P], compare_op=ALU.is_ge, fill=fill, base=0,
                               pattern=[[-1, P]], channel_multiplier=1)
            pool.affine_select(out=out[:, P:3 * P], in_=in_[:, P:3 * P], compare_op=ALU.is_ge, fill=fill, base=P,
                               pattern=[[-1, T]], channel_multiplier=1).then_inc(done, 1)

        pool.wait_ge(sem("idx_added"), IDX_H)
        drop_hidden(sel_work, score, HIDDEN, sem("hidden_dropped"))
        pool.wait_ge(sem("selected"), 1)
        drop_hidden(keep, score, 0.0, sem("keep_ready"))

        pool.wait_ge(sem("gla_operand"), GLA_H)
        pool.dma_start(memN, a["mem"][0].rearrange("(t p) d -> p t d", p=P)).then_inc(sem("mem_landed"), 16)
        pool.wait_ge(sem("cross_out_high"), XH)
        pool.dma_start(skN, a["peer_sub_keys"][0].rearrange("h s n d -> n (h s) d")).then_inc(sem("keys_landed"), 16)
        pool.wait_ge(sem("h3_scaled"), 4)
        pool.wait_ge(sem("h_rows"), 8)
        for t in range(TT):
            pool.dma_start(xnN[:, t], a["norm_ffn_g"][0].partition_broadcast(P)).then_inc(sem("ffn_gain_landed"), 16)
        pool.wait_ge(sem("sims_ready"), PEER_H)
        pool.dma_start(gfin, a["norm_final_g"].partition_broadcast(P)).then_inc(sem("final_gain_landed"), 16)

        u_rows, v_rows = a["peer_u"][0], a["peer_v"][0]

        def stage(g, slot):
            pool.wait_ge(sem("routed"), g + 1)
            wait(pool, sem("v_used"), (g - 3) * PTOP)
            pool.tensor_copy(stage_idx[:, slot], idx_all[:, bass.ds(g * PTOP, PTOP)]).then_inc(sem("idx_staged"), 1)
            pool.wait_ge(sem("idx_staged"), g + 1)

        def gather(table, rows, landed, slot, k):
            pool.indirect_dma_start(rows[:, k % RING], None, table,
                                    bass.IndirectOffsetOnAxis(ap=stage_idx[:, slot, k:k + 1], axis=0)
                                    ).then_inc(landed[k % RING], 16)

        def gather_u(g, slot, k):
            apart(sem("dotted"), g * PTOP + (k - RING + 1))
            gather(u_rows, urow, u_landed, slot, k)

        def gather_v(g, slot, k):
            apart(sem("v_used"), g * PTOP + (k - RING + 1))
            gather(v_rows, vrow, v_landed, slot, k)

        def group(g, slot, last=False):
            if not last:
                stage(g + 1, (slot + 1) % 4)
            for k in range(PTOP):
                if not last:
                    gather_u(g + 1, (slot + 1) % 4, k)
                gather_v(g, slot, k)

        stage(0, 0)
        pool.wait_ge(units_used, unit(END, 0))
        for k in range(PTOP):
            gather_u(0, 0, k)
        for g in range(4):
            group(g, g)
        with pool.Fori(1, 3) as b:
            for s in range(4):
                group(b * 4 + s, s)
        for g in range(12, GROUPS):
            group(g, g % 4, last=(g == GROUPS - 1))

    @block.scalar
    def _(act):
        for dst, src in ((consts, a["consts"]),
                         (gain_rows[G_MIX:G_X], a["norm_mix_g"][0].rearrange("(k p) -> k p", p=P)),
                         (gain_rows[G_X:G_MEM], a["norm_x_g"][0].rearrange("(k p) -> k p", p=P)),
                         (gain_rows[G_MEM:G_FFN], a["norm_mem_g"][0].rearrange("(k p) -> k p", p=P)),
                         (gain_rows[G_FFN:G_HEAD], a["norm_ffn_g"][0].rearrange("(k p) -> k p", p=P)),
                         (gain_rows[G_HEAD:G_BIAS], a["gla_head_norm_g"][0].rearrange("h (k p) -> (h k) p", p=P)),
                         (gain_rows[G_BIAS:G_ROWS], a["gla_gate_b"][0].rearrange("(k p) -> k p", p=P)),
                         (pos_i, a["positions"][0].partition_broadcast(P))):
            act.dma_start(dst, src).then_inc(sem("consts_landed"), 16)
        for dst, name, w in ((0, "i_k", IDX_D), (IDX_D, "i_k", IDX_D), (P, "d_k", DH), (2 * P, "d_v", DH), (3 * P, "i_w", IDX_H),
                             (3 * P + IDX_H, "g_low", RANK)):
            act.dma_start(small_w[:, :, dst:dst + w],
                          w_in[:, COL[name]:COL[name] + w].rearrange("(k p) n -> p k n", p=P)).then_inc(sem("small_landed"), 16)
        act.wait_ge(sem("gains_turned"), 1)
        act.activation(gains, bank[7][:, 0:G_ROWS], ACT.Copy).then_inc(sem("gains_ready"), 1)
        copy_in(act, "x", hT)
        norm_squares(act, "x", hT, turned=sem("x_copied"))
        split_high(act, 0, 0)
        norm_root(act, "x")
        for n, tab in enumerate((sin_d, cos_d, sin_i, cos_i)):
            act.wait_ge(sem("angles"), n + 1)
            act.activation(tab, tab, ACT.Sin).then_inc(sem("tables"), 1)
        operand_high(act, sem("x_scaled"), "x", scr, act_hi)

        def swap_halves(src, w, done):
            for s in range(0, P, w):
                o = s ^ w
                ins = act.activation(swap[s:s + w, 0:src.shape[1]], src[o:o + w], ACT.Copy)
            ins.then_inc(done, 1)

        act.wait_ge(sem("small_done"), 5)
        act.wait_ge(sem("x_operand"), 4)
        swap_halves(bank[2][:, 0:T].unsqueeze(1), IDX_D // 2, sem("small_swapped"))
        act.wait_ge(sem("small_roped"), 1)
        swap_halves(bank[3][:, 0:T].unsqueeze(1), DH // 2, sem("small_swapped"))
        act.activation(vdN, bank[4][:, 0:TT * DH].rearrange("p (t d) -> p t d", t=TT), ACT.Copy)
        act.activation(idx_w, bank[5][:, 0:TT * IDX_H].rearrange("p (t h) -> p t h", t=TT), ACT.Copy, scale=IDX_H ** -0.5)
        act.activation(g_low[0:RANK], bank[7][0:RANK, 0:T], ACT.Copy).then_inc(sem("small_copied"), 1)

        for i in range(2):
            def swap_iq(p, c, i=i):
                multiplied(act, p, c)
                wait(act, sem("small_roped"), 2)
                wait(act, sem("iq_roped"), 2 * i + c)
                swap_halves(proj[c], IDX_D // 2, sem("iq_swapped"))
            evacuating(act, split_high, IQ + i, swap_iq)
            for hh in range(8):
                h = 8 * i + hh
                act.wait_ge(sem("idx_scored"), h + 1)
                wait(act, sem("idx_added"), h - 1)
                act.activation(relu[:, h % 2], bank[2 + h % 4][:, 0:3 * P], ACT.Relu, scale=IDX_D ** -0.5
                               ).then_inc(sem("idx_relued"), 1)

        def dsa_pair(i):
            def swap_dq(p, c):
                multiplied(act, p, c)
                wait(act, sem("dq_roped"), i * 2 + c)
                swap_halves(proj[c], DH // 2, sem("dq_swapped"))
            evacuating(act, split_high, i + DQ, swap_dq)
            for hh in range(4):
                act.wait_ge(sem("dsa_max"), i * 4 + hh + 1)
                for t, (lo, hi) in enumerate(((0, 1), (1, 3))):
                    ins = act.activation(probs[:, hh, lo:hi], probs[:, hh, lo:hi], ACT.Exp,
                                         bias=negmax[:, 2 * hh + t:2 * hh + t + 1], accum_out=psums[:, 2 * hh + t:2 * hh + t + 1])
                ins.then_inc(sem("dsa_exp"), 1)
            for hh in range(4):
                act.wait_ge(sem("dsa_turned"), i * 4 + hh + 1)
                act.activation(probs[:, hh], bank[2 + hh][:, 0:3 * P].rearrange("p (b t) -> p b t", b=3), ACT.Copy
                               ).then_inc(sem("dsa_probsT"), 1)
            for hh in range(4):
                act.wait_ge(sem("dsa_out"), i * 4 + hh + 1)
                act.activation(att_hi[:, bass.ds(i * 4 + hh, 1)], bank[6 + hh % 2][:, 0:T].unsqueeze(1), ACT.Copy
                               ).then_inc(sem("dsa_high"), 1)

        dsa_pair(0)
        with act.Fori(1, 4) as i:
            dsa_pair(i)

        def sigmoid_gate(p, c):
            multiplied(act, p, c)
            act.activation(sg[:, c], proj[c], ACT.Sigmoid).then_inc(bank_free[c], 1)

        def gates(first, lo, hi):
            with act.Fori(lo, hi) as i:
                evacuating(act, split_high, i * 2 + first, sigmoid_gate)
                evacuating(act, split_high, i * 2 + first + 1, nothing)

        gates(GB, 0, 4)

        act.wait_ge(bank_free[1], GB + 8)
        act.dma_start(w2[0:RANK], a["gla_gate_w2"][0]).then_inc(sem("w2_landed"), 16)
        act.wait_ge(sem("gate_abs"), 1)
        act.activation(ge, ge, ACT.Exp, scale=-1.0).then_inc(sem("gate_exp"), 1)
        act.wait_ge(sem("gate_exp"), 1)
        act.activation(ge, ge, ACT.Ln, bias=1.0).then_inc(sem("gate_ln"), 1)
        act.wait_ge(sem("gates_summed"), 1)

        def gla_head(h):
            def level_decays(lo, hi):
                for lev in range(lo, hi):
                    m = P >> lev
                    e = halves(decay[lev % 2], m)
                    act.wait_ge(sem("gla_diff"), h * 8 + lev + 1)
                    act.activation(e[:, :, 0], e[:, :, 0], ACT.Exp, scale=-1.0 / GATE_TEMP)
                    act.activation(e[:, :, 1], e[:, :, 1], ACT.Exp, scale=1.0 / GATE_TEMP).then_inc(sem("gla_decay"), 1)

            def evac_qk(p, c):
                multiplied(act, p, c)
                if c == 0:
                    wait(act, sem("gla_operand"), h)
                act.activation((qg, kg)[c], proj[c], ACT.Copy, scale=(DK ** -0.5, 1.0)[c]).then_inc(bank_free[c], 1)

            def evac_v(p, c):
                multiplied(act, p, c)
                act.activation(vg[:, :, c * CH:(c + 1) * CH], proj[c], ACT.Copy).then_inc(bank_free[c], 1)

            def evac_r(p, c):
                multiplied(act, p, c)
                act.activation(swish[:, 2 * c:2 * c + 2], proj[c], ACT.Silu).then_inc(bank_free[c], 1)

            p = h * 3 + GL
            evacuating(act, split_high, p, evac_qk)
            level_decays(0, 3)
            split_high(act, p + 1, 1)
            evac_v(p + 1, 0)
            level_decays(3, 6)
            split_high(act, p + 2, 0)
            evac_v(p + 1, 1)
            level_decays(6, 8)
            evacuating(act, split_high, p + 2, evac_r)
            act.wait_ge(sem("gla_out"), h + 1)
            act.wait_ge(sem("gla_attn"), h + 1)
            for n in range(2):
                act.activation(osq[:, 2 * n:2 * n + 2], bank[6 + n].rearrange("p (e t) -> p e t", e=2), ACT.Square
                               ).then_inc(sem("gla_squares"), 1)
            act.wait_ge(sem("gla_sums"), h + 1)
            act.activation(rstd, bank[5][:, 0:T], ACT.Sqrt, scale=1.0 / DV, bias=const(EPSC)).then_inc(sem("gla_root"), 1)
            act.wait_ge(sem("gla_gated"), h + 1)
            act.activation(att_hi[:, bass.ds(h * 4, 4)], onorm, ACT.Copy).then_inc(sem("gla_high"), 1)

        gla_head(0)
        with act.Fori(1, GLA_H) as h:
            gla_head(h)

        gates(GA, 0, 2)
        copy_in(act, "mem", memT)
        norm_squares(act, "mem", memT, turned=sem("mem_copied"))
        norm_root(act, "mem")
        gates(GA, 2, 4)
        act.wait_ge(units_used, unit(XK, 0))
        operand_high(act, sem("mem_scaled"), "mem", scr, att_hi)
        act.wait_ge(bank_free[1], XK)
        operand_high(act, None, "merged", merged, act_hi)
        act.wait_ge(sem("merged_operand"), 4)

        def copy_out(dst, lead):
            def evac(p, c):
                multiplied(act, p, c)
                act.activation(dst(p - lead, c), proj[c], ACT.Copy).then_inc(bank_free[c], 1)
            return evac

        def run(first, lo, hi, evac):
            with act.Fori(lo, hi) as i:
                evacuating(act, split_high, i + first, evac)

        def keys_at(i, c):
            return kcT[:, bass.ds(i * 4 + 2 * c, 2)]

        def values_at(i, c):
            return vcN[:, :, bass.ds(i * 2 * CH + c * CH, CH)]

        run(XK, 0, 4, copy_out(keys_at, XK))
        run(WO, 0, 4, nothing)
        act.wait_ge(bank_free[1], XV)
        norm_squares(act, "h2", hT)
        run(XV, 0, 1, copy_out(values_at, XV))
        norm_root(act, "h2")
        operand_high(act, sem("h2_scaled"), "h2", scr, act_hi)
        run(XV, 1, 4, copy_out(values_at, XV))

        def query_at(i, c):
            return qx[:, 2 * c:2 * c + 2]

        act.wait_ge(sem("h2_operand"), 4)
        for i in range(XH):
            wait(act, sem("cross_scored"), 2 * i)
            evacuating(act, split_high, XQ + i, copy_out(query_at, XQ))
            for t in range(TT):
                act.wait_ge(sem("cross_max"), i + 1)
                ins = act.activation(px[:, t], bank[2].rearrange("p (t m) -> p t m", t=TT)[:, t], ACT.Exp, scale=XD ** -0.5,
                                     bias=negmax[:, t:t + 1], accum_out=psums[:, t:t + 1])
            ins.then_inc(sem("cross_exp"), 1)
            act.wait_ge(sem("cross_turned"), i + 1)
            act.activation(pxT, bank[3].rearrange("p (m t) -> p m t", m=2), ACT.Copy).then_inc(sem("cross_probsT"), 1)
            act.wait_ge(sem("cross_out"), i + 1)
            for n in range(2):
                ins = act.activation(att_hi[:, 4 * i + 2 * n:4 * i + 2 * n + 2], bank[6 + n].rearrange("p (e t) -> p e t", e=2),
                                     ACT.Copy)
            ins.then_inc(sem("cross_out_high"), 1)

        run(XO, 0, 2, nothing)
        for n in range(4):
            act.wait_ge(sem("keys_turned"), n + 1)
            act.activation(skT[:, 4 * n:4 * n + 4], bank[2 + n].rearrange("p (g n) -> p g n", g=4), ACT.Copy
                           ).then_inc(sem("keys_ready"), 1)
        run(XO, 2, 4, nothing)
        act.wait_ge(bank_free[1], PQ)
        norm_squares(act, "h3", hT)
        for j in range(8):
            act.wait_ge(sem("rows_turned"), j + 1)
            act.activation(hN[:, j // 4, (j % 4) * 512:(j % 4 + 1) * 512], bank[2 + j % 4], ACT.Copy).then_inc(sem("h_rows"), 1)
        norm_root(act, "h3")
        operand_high(act, sem("h3_scaled"), "h3", scr, act_hi)
        for t in range(TT):
            act.wait_ge(sem("h_rows"), 8)
            act.wait_ge(sem("h3_operand"), 4)
            act.activation(scr.rearrange("p k t -> p (k t)")[:, t * D:(t + 1) * D], hN[:, t], ACT.Square, accum_out=gsum[:, t:t + 1]
                           ).then_inc(sem("row_squares"), 1)
        act.wait_ge(sem("row_squares"), 2)
        act.activation(stat[:, 0:2], gsum[:, 0:2], ACT.Sqrt, scale=1.0 / D, bias=const(EPSC)).then_inc(sem("row_root"), 1)

        def peer_pair(p, i, last=False):
            def evac(p, c):
                multiplied(act, p, c)
                wait(act, sem("peer_scored"), i * 2 - 2 + c + 1)
                act.activation(qp[:, c], proj[c], ACT.Copy).then_inc(bank_free[c], 1)
            evacuating(act, split_high, p, evac, last)
            for c in range(2):
                act.wait_ge(sem("peer_scored"), i * 2 + c + 1)
                view = bank[2 + c].rearrange("p (s t n) -> p s t n", s=2, t=TT)
                for t in range(TT):
                    dst = sims[:, bass.ds(i * 2 + (t * PEER_H + c), 1)].rearrange("p g s n -> p (g s) n")
                    ins = act.activation(dst, view[:, :, t], ACT.Copy)
                ins.then_inc(sem("sims_ready"), 1)

        act.wait_ge(sem("keys_ready"), 4)
        peer_pair(PQ, 0)
        with act.Fori(1, 3) as i:
            peer_pair(i + PQ, i)
        peer_pair(PQ + 3, 3, last=True)

        def gate_exp(g):
            act.wait_ge(sem("cands_ready"), g + 1)
            act.activation(egate, cv, ACT.Exp, bias=stat[:, 4:5], accum_out=stat[:, 5:6]).then_inc(sem("gate_exped"), 1)

        def diagonals(g, lo, hi):
            for k in range(lo, hi):
                wait(act, sem("v_used"), g * PTOP + (k - 3))
                act.activation(diag[:, k % 4], ident, ACT.Copy, scale=wexp[:, k:k + 1]).then_inc(sem("diag_ready"), 1)

        def expert_weights(g, between=()):
            act.wait_ge(sem("dotted"), g * PTOP + PTOP)
            act.activation(gelu, dots, ACT.Gelu_apprx_tanh).then_inc(sem("gelu_ready"), 1)
            act.wait_ge(sem("weights_ready"), g + 1)
            diagonals(g, 0, 4)
            for step, arg in between:
                step(arg)
            diagonals(g, 4, PTOP)

        def finish(t):
            act.wait_ge(sem("v_used"), (t + 1) * PEER_H * PTOP)
            for n in range(4):
                ins = act.activation(hN[:, t, n * 512:(n + 1) * 512], bank[4 * t + n], ACT.Square, accum_out=gsum[:, n:n + 1])
            ins.then_inc(sem("out_squares"), 1)
            act.wait_ge(sem("out_summed"), t + 1)
            act.activation(stat[:, 6:7], stat[:, 6:7], ACT.Sqrt, scale=1.0 / D, bias=const(EPSC)).then_inc(sem("out_root"), 1)

        gate_exp(0)
        gate_exp(1)
        expert_weights(0, [(gate_exp, 2)])
        with act.Fori(1, 8) as g:
            expert_weights(g, [(gate_exp, g + 2)])
        expert_weights(8, [(gate_exp, 10), (finish, 0)])
        with act.Fori(9, 14) as g:
            expert_weights(g, [(gate_exp, g + 2)])
        expert_weights(14)
        expert_weights(15)
        finish(1)

    @block.tensor
    def _(pe):
        pe.wait_ge(sem("consts_landed"), 16 * 8)
        pe.transpose(bank[7][:, 0:G_ROWS], gain_rows[0:G_ROWS], ident[0:G_ROWS, 0:G_ROWS]).then_inc(sem("gains_turned"), 1)
        pe.wait_ge(sem("x_landed"), 16)
        turn_in(pe, "x", xN)
        pe.wait_ge(sem("ones_ready"), 1)
        norm_sums(pe, "x")

        pe.wait_ge(sem("small_landed"), 16 * 6)
        pe.wait_ge(sem("x_scaled"), 4)
        pe.wait_ge(sem("x_copied"), 8)
        pe.wait_ge(sem("gains_ready"), 1)

        def small(out, lhs, rhs):
            for k in range(KT):
                mm = pe.matmul(out, lhs(k), rhs(k), start=(k == 0), stop=(k == KT - 1))
            return mm

        small(bank[2][:, 0:T], lambda k: small_w[:, k, 0:P], lambda k: scr[:, k]).then_inc(sem("small_done"), 1)
        small(bank[3][:, 0:T], lambda k: small_w[:, k, P:2 * P], lambda k: scr[:, k]).then_inc(sem("small_done"), 1)
        for t in range(TT):
            mm = small(bank[4][:, t * DH:(t + 1) * DH], lambda k: scr[:, k, t * P:(t + 1) * P],
                       lambda k: small_w[:, k, 2 * P:3 * P])
        mm.then_inc(sem("small_done"), 1)
        for t in range(TT):
            mm = small(bank[5][:, t * IDX_H:(t + 1) * IDX_H], lambda k: scr[:, k, t * P:(t + 1) * P],
                       lambda k: small_w[:, k, 3 * P:3 * P + IDX_H])
        mm.then_inc(sem("small_done"), 1)
        small(bank[7][0:RANK, 0:T], lambda k: small_w[:, k, 3 * P + IDX_H:], lambda k: scr[:, k]).then_inc(sem("small_done"), 1)

        pe.wait_ge(sem("x_operand"), 4)
        for i in range(2):
            for c in range(2):
                multiply(pe, IQ + i, c, act_hi, act_lo)
            if i == 0:
                pe.wait_ge(sem("small_roped"), 2)
                pe.wait_ge(sem("small_copied"), 1)
            for hh in range(8):
                h = 8 * i + hh
                pe.wait_ge(sem("iq_roped"), h // 4 + 1)
                wait(pe, sem("idx_relued"), h - 3)
                c, n, s = hh // 4, hh // 2 % 2, slice(IDX_D * (hh % 2), IDX_D * (hh % 2 + 1))
                b = bank[2 + h % 4]
                pe.matmul(b[:, 0:P], qbuf[s, c, n, 0:P], kiT[s, 0:P], start=True, stop=True)
                pe.matmul(b[:, P:3 * P], qbuf[s, c, n, P:T], kiT[s], start=True, stop=True).then_inc(sem("idx_scored"), 1)

        def dsa_pair(i):
            for c in range(2):
                multiply(pe, i + DQ, c, act_hi, act_lo)
            for hh in range(4):
                pe.wait_ge(sem("dq_roped"), i * 2 + (hh // 2 + 1))
                q, b = qbuf[:, hh // 2, hh % 2], bank[2 + hh]
                pe.matmul(b[:, 0:P], q[:, 0:P], kdT[:, 0:P], start=True, stop=True)
                pe.matmul(b[:, P:3 * P], q[:, P:T], kdT, start=True, stop=True).then_inc(sem("dsa_logits"), 1)
            for hh in range(4):
                pe.wait_ge(sem("dsa_probs"), i * 4 + hh + 1)
                for n, dst in enumerate((0, 1, 2)):
                    mm = pe.transpose(bank[2 + hh][:, dst * P:(dst + 1) * P], probs[:, hh, n], ident)
                mm.then_inc(sem("dsa_turned"), 1)
            for hh in range(4):
                pe.wait_ge(sem("dsa_probsT"), i * 4 + hh + 1)
                wait(pe, sem("dsa_operand"), i * 4 + hh - 1)
                b = bank[6 + hh % 2]
                pe.matmul(b[:, 0:T], vdN[:, 0], probs[:, hh, 0:2], start=True, stop=False, skip_group_check=True)
                pe.matmul(b[:, P:T], vdN[:, 1], probs[:, hh, 2], start=False, stop=True, skip_group_check=True
                          ).then_inc(sem("dsa_out"), 1)

        dsa_pair(0)
        with pe.Fori(1, 4) as i:
            dsa_pair(i)

        pe.wait_ge(sem("dsa_operand"), DSA_H)

        def gated(first, lo, hi):
            with pe.Fori(lo, hi) as i:
                for c in range(2):
                    multiply(pe, i * 2 + first, c, act_hi, act_lo)
                for c in range(2):
                    multiply(pe, i * 2 + first + 1, c, att_hi, att_lo)

        gated(GB, 0, 4)

        pe.wait_ge(sem("w2_landed"), 16)
        for n in range(8):
            mm = pe.matmul(bank[2 + n // 2][:, (n % 2) * T:(n % 2 + 1) * T], w2[0:RANK, n * P:(n + 1) * P], g_low[0:RANK],
                           start=True, stop=True)
        mm.then_inc(sem("gate_logits"), 1)
        pe.wait_ge(sem("gate_biased"), 1)
        def gla_head(h):
            def scores(lo, hi):
                for lev in range(lo, hi):
                    b = bank[2 + lev % 3]
                    if lev < 8:
                        pe.wait_ge(sem("gla_z"), h * 8 + lev + 1)
                    wait(pe, sem("gla_added"), h * 9 + lev - 2)
                    z = zlev[lev % 3] if lev < 8 else None
                    for blk in range(1 if lev == 0 else 2):
                        s = slice(blk * P, (blk + 1) * P)
                        for d in range(2):
                            lhs, rhs = (kg[:, d, s], qg[:, d, s]) if lev == 8 else (
                                z[:, d, s], z[:, d, P:T] if lev == 0 else z[:, d, s])
                            mm = pe.matmul(b[:, s], lhs, rhs, start=(d == 0), stop=(d == 1))
                    mm.then_inc(sem("gla_scored"), 1)

            p = h * 3 + GL
            multiply(pe, p, 0, act_hi, act_lo)
            multiply(pe, p, 1, act_hi, act_lo)
            multiply(pe, p + 1, 0, act_hi, act_lo, tokens_out=True)
            scores(0, 3)
            multiply(pe, p + 1, 1, act_hi, act_lo, tokens_out=True)
            scores(3, 6)
            multiply(pe, p + 2, 0, act_hi, act_lo)
            scores(6, 9)
            multiply(pe, p + 2, 1, act_hi, act_lo)
            pe.wait_ge(sem("gla_attn"), h + 1)
            wait(pe, sem("gla_operand"), h)
            for e in range(4):
                b, o = bank[6 + e // 2], (e % 2) * T
                pe.matmul(b[:, o:o + T], vg[:, 0, e * P:(e + 1) * P], attn[:, 0:2], start=True, stop=False,
                          skip_group_check=True)
                mm = pe.matmul(b[:, o + P:o + T], vg[:, 1, e * P:(e + 1) * P], attn[:, 2], start=False, stop=True,
                               skip_group_check=True)
            mm.then_inc(sem("gla_out"), 1)
            for e in range(4):
                pe.wait_ge(sem("gla_squares"), h * 2 + e // 2 + 1)
                mm = pe.matmul(bank[5][:, 0:T], ones[:, 0:P], osq[:, e], start=(e == 0), stop=(e == 3))
            mm.then_inc(sem("gla_sums"), 1)

        gla_head(0)
        with pe.Fori(1, GLA_H) as h:
            gla_head(h)

        pe.wait_ge(sem("gla_operand"), GLA_H)
        gated(GA, 0, 2)
        pe.wait_ge(sem("mem_landed"), 16)
        turn_in(pe, "mem", memN)
        norm_sums(pe, "mem")
        gated(GA, 2, 4)

        def run(first, lo, hi, hi_op, lo_op, tokens_out=False):
            with pe.Fori(lo, hi) as i:
                for c in range(2):
                    multiply(pe, i + first, c, hi_op, lo_op, tokens_out)

        pe.wait_ge(sem("mem_operand"), 4)
        run(XK, 0, 4, att_hi, att_lo)
        pe.wait_ge(sem("merged_operand"), 4)
        run(WO, 0, 4, act_hi, act_lo)
        run(XV, 0, 1, att_hi, att_lo, True)
        norm_sums(pe, "h2")
        run(XV, 1, 4, att_hi, att_lo, True)

        pe.wait_ge(sem("h2_operand"), 4)
        for h in range(XH):
            multiply(pe, XQ + h, 0, act_hi, act_lo)
            multiply(pe, XQ + h, 1, act_hi, act_lo)
            pe.wait_ge(bank_free[1], XQ + h + 1)
            for t in range(TT):
                for k in range(4):
                    mm = pe.matmul(bank[2][:, t * T:(t + 1) * T], qx[:, k, t * P:(t + 1) * P], kcT[:, 4 * h + k], start=(k == 0),
                                   stop=(k == 3))
                mm.then_inc(sem("cross_scored"), 1)
            pe.wait_ge(sem("cross_probs"), h + 1)
            for m in range(2):
                for t in range(TT):
                    mm = pe.transpose(bank[3][:, m * T + t * P:m * T + (t + 1) * P], px[:, t, m * P:(m + 1) * P], ident)
            mm.then_inc(sem("cross_turned"), 1)
            pe.wait_ge(sem("cross_probsT"), h + 1)
            wait(pe, sem("cross_operand"), h)
            for e in range(4):
                for m in range(2):
                    o = h * XD + e * P
                    mm = pe.matmul(bank[6 + e // 2][:, (e % 2) * T:(e % 2 + 1) * T], vcN[:, m, o:o + P], pxT[:, m],
                                   start=(m == 0), stop=(m == 1))
            mm.then_inc(sem("cross_out"), 1)

        pe.wait_ge(sem("cross_operand"), XH)
        run(XO, 0, 2, att_hi, att_lo)
        pe.wait_ge(sem("keys_landed"), 16)
        for g in range(2 * PEER_H):
            mm = pe.transpose(bank[2 + g // 4][:, (g % 4) * P:(g % 4 + 1) * P], skN[:, g], ident)
            if g % 4 == 3:
                mm.then_inc(sem("keys_turned"), 1)
        run(XO, 2, 4, att_hi, att_lo)
        pe.wait_ge(bank_free[1], PQ)
        pe.wait_ge(sem("keys_ready"), 4)
        for j in range(8):
            if j >= 4:
                pe.wait_ge(sem("h_rows"), j - 3)
            t = j // 4
            for k in range(4):
                mm = pe.transpose(bank[2 + j % 4][:, k * P:(k + 1) * P], hT[:, (j % 4) * 4 + k, t * P:(t + 1) * P], ident)
            mm.then_inc(sem("rows_turned"), 1)
        norm_sums(pe, "h3")
        pe.wait_ge(sem("h3_operand"), 4)
        def peer_pair(i):
            for c in range(2):
                multiply(pe, i + PQ, c, act_hi, act_lo)
            for c in range(2):
                pe.wait_ge(bank_free[c], i + PQ + 1)
                wait(pe, sem("sims_ready"), i * 2 + c - 1)
                for s in range(2):
                    for t in range(TT):
                        o = (s * TT + t) * NKEYS
                        mm = pe.matmul(bank[2 + c][:, o:o + NKEYS], qp[:, c, s, t * P:(t + 1) * P],
                                       skT[:, bass.ds(i * 4 + 2 * c + s, 1)].rearrange("p g n -> p (g n)"), start=True, stop=True)
                mm.then_inc(sem("peer_scored"), 1)

        peer_pair(0)
        with pe.Fori(1, 4) as i:
            peer_pair(i)

        def seed(t):
            for n in range(4):
                pe.matmul(bank[4 * t + n], ident, hN[:, t, n * 512:(n + 1) * 512], start=True, stop=False,
                          skip_group_check=True)

        def value_rows(g, t, last=False):
            for k in range(PTOP):
                pe.wait_ge(sem("diag_ready"), g * PTOP + k + 1)
                pe.wait_ge(v_landed[k % RING], g * 32 + (k // RING + 1) * 16)
                for n in range(4):
                    mm = pe.matmul(bank[4 * t + n], diag[:, k % 4], vrow[:, k % RING, n * 512:(n + 1) * 512], start=False,
                                   stop=(last and k == PTOP - 1), skip_group_check=True)
                mm.then_inc(sem("v_used"), 1)

        pe.wait_ge(sem("sims_ready"), PEER_H)
        for t in range(TT):
            seed(t)
            with pe.Fori(t * PEER_H, (t + 1) * PEER_H - 1) as g:
                value_rows(g, t)
            value_rows((t + 1) * PEER_H - 1, t, last=True)

    @block.vector
    def _(dve):
        link = Chain(dve, sem("vector_step"), Apart(dve, sem("ones_ready")))
        dve.memset(ones, 1.0).then_inc(sem("ones_ready"), 1)

        dve.wait_ge(sem("consts_landed"), 16 * 8)
        link(dve.tensor_copy(pos_f, pos_i))
        for inv, sin_t, cos_t in ((INV_D, sin_d, cos_d), (INV_I, sin_i, cos_i)):
            link(dve.tensor_scalar(angle, pos_f, const(inv), None, ALU.mult))
            for tab, shift in ((sin_t, 0.0), (cos_t, 0.25)):
                link(dve.tensor_scalar(turns, angle, 1.0 / (2 * np.pi), shift, ALU.mult, ALU.add))
                link(dve.tensor_scalar(turns, turns, ROUND, None, ALU.add))
                link(dve.tensor_scalar(turns, turns, ROUND, None, ALU.subtract))
                link(dve.scalar_tensor_tensor(out=tab, in0=turns, scalar=-TWO_PI_1, in1=angle, op0=ALU.mult, op1=ALU.add))
                link(dve.scalar_tensor_tensor(out=tab, in0=turns, scalar=-TWO_PI_2, in1=tab, op0=ALU.mult, op1=ALU.add))
                link(dve.scalar_tensor_tensor(out=tab, in0=turns, scalar=-TWO_PI_3, in1=tab, op0=ALU.mult, op1=ALU.add))
                link(dve.tensor_scalar(tab, tab, shift * 2 * np.pi, PI, ALU.add, ALU.min))
                dve.tensor_scalar(tab, tab, -PI, None, ALU.max).then_inc(sem("angles"), 1)

        dve.wait_ge(sem("gains_ready"), 1)
        split_low(dve, 0, 0)
        norm_scale(dve, link, "x", hT, G_MIX)
        dve.wait_ge(sem("tables"), 4)
        for tab, sgn in ((sin_d, SGN_D), (sin_i, SGN_I)):
            link(dve.tensor_scalar(tab, tab, const(sgn), None, ALU.mult))
        operand_low(dve, "x", scr, act_hi, act_lo)

        def rope(src, n, cos_t, sin_t, out, done, bank_done=None):
            wide = [P, n, T]
            ins = dve.tensor_tensor(rot[:, 0:n], src, cos_t.unsqueeze(1).broadcast_to(wide), ALU.mult)
            if bank_done is not None:
                ins.then_inc(bank_done, 1)
            link(dve.tensor_tensor(swap[:, 0:n], swap[:, 0:n], sin_t.unsqueeze(1).broadcast_to(wide), ALU.mult))
            dve.tensor_tensor(out, rot[:, 0:n], swap[:, 0:n], ALU.add).then_inc(done, 1)

        dve.wait_ge(sem("small_swapped"), 1)
        rope(bank[2][:, 0:T].unsqueeze(1), 1, cos_i, sin_i, kiT.unsqueeze(1), sem("small_roped"))
        dve.wait_ge(sem("small_swapped"), 2)
        rope(bank[3][:, 0:T].unsqueeze(1), 1, cos_d, sin_d, kdT.unsqueeze(1), sem("small_roped"))

        for i in range(2):
            def rope_iq(p, c, i=i):
                dve.wait_ge(sem("iq_swapped"), 2 * i + c + 1)
                wait(dve, sem("idx_scored"), 8 * i - 8 + 4 * c + 4)
                rope(proj[c], 2, cos_i, sin_i, qbuf[:, c], sem("iq_roped"), bank_free[c])
            evacuating(dve, split_low, IQ + i, rope_iq)
            if i == 0:
                dve.wait_ge(sem("small_copied"), 1)
            for hh in range(8):
                h = 8 * i + hh
                dve.wait_ge(sem("idx_relued"), h + 1)
                if h:
                    dve.wait_ge(sem("idx_added"), h)
                for t, (lo, hi) in enumerate(((0, P), (P, 3 * P))):
                    w = idx_w[:, t, h:h + 1]
                    if h == 0:
                        ins = dve.tensor_scalar(score[:, lo:hi], relu[:, 0, lo:hi], w, None, ALU.mult)
                    else:
                        ins = dve.scalar_tensor_tensor(out=score[:, lo:hi], in0=relu[:, h % 2, lo:hi], scalar=w,
                                                       in1=score[:, lo:hi], op0=ALU.mult, op1=ALU.add)
                ins.then_inc(sem("idx_added"), 1)
        dve.wait_ge(sem("hidden_dropped"), 1)
        for lo, hi in ((0, P), (P, 3 * P)):
            for _ in range(TOPK // 8):
                link(dve.max(top8, sel_work[:, lo:hi]))
                link(dve.match_replace(sel_work[:, lo:hi], top8, sel_work[:, lo:hi], TAKEN))
        dve.tensor_scalar(score, sel_work, 2 * HIDDEN, None, ALU.is_le).then_inc(sem("selected"), 1)
        dve.wait_ge(sem("keep_ready"), 1)
        link(dve.tensor_scalar(keep, keep, 1.0, -NEG, ALU.subtract, ALU.mult))

        def dsa_pair(i):
            def rope_dq(p, c):
                dve.wait_ge(sem("dq_swapped"), i * 2 + c + 1)
                rope(proj[c], 2, cos_d, sin_d, qbuf[:, c], sem("dq_roped"), bank_free[c])
            evacuating(dve, split_low, i + DQ, rope_dq)
            for hh in range(4):
                dve.wait_ge(sem("dsa_logits"), i * 4 + hh + 1)
                link(dve.scalar_tensor_tensor(out=probs[:, hh].rearrange("p b k -> p (b k)"), in0=bank[2 + hh][:, 0:3 * P],
                                              scalar=DH ** -0.5, in1=keep, op0=ALU.mult, op1=ALU.add))
                for t, (lo, hi) in enumerate(((0, 1), (1, 3))):
                    ins = dve.tensor_reduce(negmax[:, 2 * hh + t:2 * hh + t + 1],
                                            probs[:, hh, lo:hi].rearrange("p b k -> p (b k)"), AX.X, ALU.max)
                link(ins)
                dve.tensor_scalar(negmax[:, 2 * hh:2 * hh + 2], negmax[:, 2 * hh:2 * hh + 2], -1.0, None, ALU.mult
                                  ).then_inc(sem("dsa_max"), 1)
            for hh in range(4):
                dve.wait_ge(sem("dsa_exp"), i * 4 + hh + 1)
                link(dve.reciprocal(prec[:, 2 * hh:2 * hh + 2], psums[:, 2 * hh:2 * hh + 2]))
                for t, (lo, hi) in enumerate(((0, 1), (1, 3))):
                    ins = dve.tensor_scalar(probs[:, hh, lo:hi], probs[:, hh, lo:hi], prec[:, 2 * hh + t:2 * hh + t + 1], None,
                                            ALU.mult)
                ins.then_inc(sem("dsa_probs"), 1)
            for hh in range(4):
                dve.wait_ge(sem("dsa_high"), i * 4 + hh + 1)
                o = bass.ds(i * 4 + hh, 1)
                dve.tensor_tensor(att_lo[:, o], bank[6 + hh % 2][:, 0:T].unsqueeze(1), att_hi[:, o].bitcast(F32), ALU.subtract
                                  ).then_inc(sem("dsa_operand"), 1)

        dsa_pair(0)
        with link.loop(1, 4, DSA_PER) as i:
            dsa_pair(i)

        with dve.Fori(0, 4) as i:
            def merge_b(p, c):
                multiplied(dve, p, c)
                dve.tensor_tensor(merged[:, bass.ds(i * 4 + 2 * c, 2)], proj[c], sg[:, c], ALU.mult).then_inc(bank_free[c], 1)
            evacuating(dve, split_low, i * 2 + GB, nothing)
            evacuating(dve, split_low, i * 2 + GB + 1, merge_b)

        dve.wait_ge(sem("gate_logits"), 1)
        for n in range(8):
            ins = dve.tensor_scalar(gz[:, n], bank[2 + n // 2][:, (n % 2) * T:(n % 2 + 1) * T],
                                    gains[:, G_BIAS + n:G_BIAS + n + 1], None, ALU.add)
        ins.then_inc(sem("gate_biased"), 1)
        dve.wait_ge(sem("gate_biased"), 1)
        flat = "p n t -> p (n t)"
        dve.scalar_tensor_tensor(out=ge.rearrange(flat), in0=gz.rearrange(flat), scalar=-1.0, in1=gz.rearrange(flat),
                                 op0=ALU.mult, op1=ALU.max).then_inc(sem("gate_abs"), 1)
        dve.wait_ge(sem("gate_ln"), 1)
        link(dve.scalar_tensor_tensor(out=gz.rearrange(flat), in0=gz.rearrange(flat), scalar=0.0, in1=ge.rearrange(flat),
                                      op0=ALU.min, op1=ALU.subtract))
        for n in range(8):
            ins = dve.tensor_tensor_scan(cum[:, n], ones, gz[:, n], 0.0, ALU.mult, ALU.add)
        ins.then_inc(sem("gates_summed"), 1)
        dve.wait_ge(sem("gates_summed"), 1)

        def gla_head(h):
            def level_diff(lev):
                m = P >> lev
                blocks = "p a (n m) -> p (a n) m"
                c = cum[:, bass.ds(h * 2, 2)].rearrange(blocks, m=2 * m)
                dve.tensor_tensor(decay[lev % 2].rearrange(blocks, m=2 * m), c, c[:, :, m - 1:m].broadcast_to([P, T // m, 2 * m]),
                                  ALU.subtract).then_inc(sem("gla_diff"), 1)

            def level_z(lev):
                m = P >> lev
                dve.wait_ge(sem("gla_decay"), h * 8 + lev + 1)
                wait(dve, sem("gla_scored"), h * 9 + lev - 2)
                for f, x in ((0, kg), (1, qg)):
                    z, x, e = (halves(y, m)[:, :, f] for y in (zlev[lev % 3], x, decay[lev % 2]))
                    ins = dve.tensor_tensor(z, x, e, ALU.mult)
                ins.then_inc(sem("gla_z"), 1)

            def levels_ahead(lo, hi):
                for lev in range(lo, hi):
                    level_diff(lev)
                    level_z(lev)

            def levels_added(lo, hi):
                for lev in range(lo, hi):
                    dve.wait_ge(sem("gla_scored"), h * 9 + lev + 1)
                    b = bank[2 + lev % 3]
                    if lev == 0:
                        dve.tensor_copy(attn[:, 1], b[:, 0:P]).then_inc(sem("gla_added"), 1)
                        continue
                    m = (mask(lev - 1) if lev < 8 else ident).unsqueeze(1).broadcast_to([P, 2, P])
                    src = b[:, 0:T].rearrange("p (b i) -> p b i", b=2)
                    if lev == 1:
                        dve.tensor_tensor(attn[:, 0:3:2], src, m, ALU.mult).then_inc(sem("gla_added"), 1)
                        continue
                    dve.tensor_tensor(masked, src, m, ALU.mult).then_inc(sem("gla_added"), 1)
                    dve.wait_ge(sem("gla_added"), h * 9 + lev + 1)
                    ins = dve.tensor_tensor(attn[:, 0:3:2], attn[:, 0:3:2], masked, ALU.add)
                    if lev == 8:
                        ins.then_inc(sem("gla_attn"), 1)
                    else:
                        link(ins)

            p = h * 3 + GL
            evacuating(dve, split_low, p, nothing)
            dve.wait_ge(bank_free[1], p + 1)
            levels_ahead(0, 3)
            split_low(dve, p + 1, 1)
            levels_added(0, 3)
            levels_ahead(3, 6)
            split_low(dve, p + 2, 0)
            levels_added(3, 6)
            levels_ahead(6, 8)
            split_low(dve, p + 2, 1)
            levels_added(6, 9)
            split_low(dve, p + 3, 0)
            dve.wait_ge(sem("gla_root"), h + 1)
            link(dve.reciprocal(rstd, rstd))
            for e in range(4):
                ins = dve.scalar_tensor_tensor(out=onorm[:, e], in0=bank[6 + e // 2][:, (e % 2) * T:(e % 2 + 1) * T],
                                               scalar=gains[:, bass.ds(h * 4 + G_HEAD + e, 1)], in1=rstd, op0=ALU.mult,
                                               op1=ALU.mult)
            link(ins)
            dve.wait_ge(bank_free[1], p + 3)
            dve.tensor_tensor(onorm, onorm, swish, ALU.mult).then_inc(sem("gla_gated"), 1)
            dve.wait_ge(sem("gla_high"), h + 1)
            o = bass.ds(h * 4, 4)
            dve.tensor_tensor(att_lo[:, o], onorm, att_hi[:, o].bitcast(F32), ALU.subtract).then_inc(sem("gla_operand"), 1)

        gla_head(0)
        with link.loop(1, GLA_H, GLA_PER) as h:
            gla_head(h)

        def branch_a(lo, hi):
            with link.loop(lo, hi, 2) as i:
                def merge_a(p, c):
                    multiplied(dve, p, c)
                    link(dve.tensor_tensor(sg[:, c], proj[c], sg[:, c], ALU.mult))
                    m = merged[:, bass.ds(i * 4 + 2 * c, 2)]
                    dve.tensor_tensor(m, m, sg[:, c], ALU.add).then_inc(bank_free[c], 1)
                evacuating(dve, split_low, i * 2 + GA, nothing)
                evacuating(dve, split_low, i * 2 + GA + 1, merge_a)

        branch_a(0, 2)
        norm_scale(dve, link, "mem", memT, G_MEM)
        branch_a(2, 4)
        operand_low(dve, "mem", scr, att_hi, att_lo)
        operand_low(dve, "merged", merged, act_hi, act_lo)

        def run(first, lo, hi, evac=None):
            with dve.Fori(lo, hi) as i:
                def add_residual(p, c):
                    multiplied(dve, p, c)
                    r = hT[:, bass.ds(i * 4 + 2 * c, 2)]
                    dve.tensor_tensor(r, r, proj[c], ALU.add).then_inc(bank_free[c], 1)
                evacuating(dve, split_low, i + first, evac or add_residual)

        run(XK, 0, 4, nothing)
        run(WO, 0, 4)
        run(XV, 0, 1, nothing)
        norm_scale(dve, link, "h2", hT, G_X)
        operand_low(dve, "h2", scr, act_hi, act_lo)
        run(XV, 1, 4, nothing)

        for h in range(XH):
            evacuating(dve, split_low, XQ + h, nothing)
            dve.wait_ge(sem("cross_scored"), 2 * h + 2)
            link(dve.tensor_reduce(negmax[:, 0:2], bank[2].rearrange("p (t m) -> p t m", t=TT), AX.X, ALU.max))
            dve.tensor_scalar(negmax[:, 0:2], negmax[:, 0:2], -(XD ** -0.5), None, ALU.mult).then_inc(sem("cross_max"), 1)
            dve.wait_ge(sem("cross_exp"), h + 1)
            link(dve.reciprocal(prec[:, 0:2], psums[:, 0:2]))
            for t in range(TT):
                ins = dve.tensor_scalar(px[:, t], px[:, t], prec[:, t:t + 1], None, ALU.mult)
            ins.then_inc(sem("cross_probs"), 1)
            dve.wait_ge(sem("cross_out_high"), h + 1)
            for n in range(2):
                o = slice(4 * h + 2 * n, 4 * h + 2 * n + 2)
                ins = dve.tensor_tensor(att_lo[:, o], bank[6 + n].rearrange("p (e t) -> p e t", e=2), att_hi[:, o].bitcast(F32),
                                        ALU.subtract)
            ins.then_inc(sem("cross_operand"), 1)

        run(XO, 0, 4)
        norm_scale(dve, link, "h3", hT, G_FFN)
        operand_low(dve, "h3", scr, act_hi, act_lo)

        dve.wait_ge(sem("row_root"), 1)
        link(dve.reciprocal(stat[:, 2:4], stat[:, 0:2]))
        dve.wait_ge(sem("ffn_gain_landed"), 16 * TT)
        for t in range(TT):
            ins = dve.scalar_tensor_tensor(out=xnN[:, t], in0=hN[:, t], scalar=stat[:, 2 + t:3 + t], in1=xnN[:, t],
                                           op0=ALU.mult, op1=ALU.mult)
        link(ins)

        run(PQ, 0, 3, nothing)
        evacuating(dve, split_low, PQ + 3, nothing, last=True)

        def top16(values, indices, src, rest):
            link(dve.max(values[:, 0:8], src))
            link(dve.max_index(indices[:, 0:8], values[:, 0:8], src))
            link(dve.match_replace(rest, values[:, 0:8], src, TAKEN))
            link(dve.max(values[:, 8:16], rest))
            link(dve.max_index(indices[:, 8:16], values[:, 8:16], rest))

        wide = [P, PTOP, PTOP]

        def route(g):
            link(dve.tensor_copy(sc, sims[:, bass.ds(g, 1)].rearrange("p g s n -> p (g s) n")))
            for s in range(2):
                top16(tv[:, s], ti[:, s], sc[:, s], sc2[:, s])
            link(dve.tensor_copy(tif, ti))
            link(dve.tensor_tensor(cand, tv[:, 0].unsqueeze(2).broadcast_to(wide), tv[:, 1].unsqueeze(1).broadcast_to(wide),
                                   ALU.add))
            wait(dve, sem("gate_exped"), g)
            top16(cv, ci, cand.rearrange("p a b -> p (a b)"), cand2.rearrange("p a b -> p (a b)"))
            dve.tensor_scalar(stat[:, 4:5], cv[:, 0:1], -1.0, None, ALU.mult).then_inc(sem("cands_ready"), 1)
            link(dve.tensor_scalar(cpart[:, 0], ci, 4, None, ALU.logical_shift_right))
            link(dve.tensor_scalar(cpart[:, 1], ci, PTOP - 1, None, ALU.bitwise_and))
            link(dve.tensor_copy(cpartf, cpart))
            for s in range(2):
                iota = consts[:, C_IOTA:C_IOTA + PTOP].unsqueeze(1).broadcast_to(wide)
                link(dve.tensor_tensor(onehot, cpartf[:, s].unsqueeze(2).broadcast_to(wide), iota, ALU.is_equal))
                link(dve.tensor_tensor(onehot, onehot, tif[:, s].unsqueeze(1).broadcast_to(wide), ALU.mult))
                link(dve.tensor_reduce(isel[:, s], onehot, AX.X, ALU.add))
            dve.scalar_tensor_tensor(out=idx_all[:, bass.ds(g * PTOP, PTOP)], in0=isel[:, 0], scalar=float(NKEYS), in1=isel[:, 1],
                                     op0=ALU.mult, op1=ALU.add).then_inc(sem("routed"), 1)
            dve.wait_ge(sem("gate_exped"), g + 1)
            link(dve.reciprocal(stat[:, 5:6], stat[:, 5:6]))
            link(dve.tensor_scalar(gates_all[:, bass.ds(g * PTOP, PTOP)], egate, stat[:, 5:6], None, ALU.mult))

        def dot_rows(g, t):
            for k in range(PTOP):
                dve.wait_ge(u_landed[k % RING], g * 32 + (k // RING + 1) * 16)
                u = urow[:, k % RING]
                dve.tensor_tensor_reduce(u, u, xnN[:, t], 1.0, 0.0, ALU.mult, ALU.add, dots[:, k:k + 1]
                                         ).then_inc(sem("dotted"), 1)
            dve.wait_ge(sem("gelu_ready"), g + 1)
            wait(dve, sem("diag_ready"), g * PTOP)
            dve.tensor_tensor(wexp, gelu, gates_all[:, bass.ds(g * PTOP, PTOP)], ALU.mult).then_inc(sem("weights_ready"), 1)

        def finish(t):
            dve.wait_ge(sem("out_squares"), t + 1)
            dve.tensor_reduce(stat[:, 6:7], gsum[:, 0:4], AX.X, ALU.add).then_inc(sem("out_summed"), 1)
            dve.wait_ge(sem("out_root"), t + 1)
            link(dve.reciprocal(stat[:, 7:8], stat[:, 6:7]))
            for n in range(4):
                s = slice(n * 512, (n + 1) * 512)
                ins = dve.scalar_tensor_tensor(out=hN[:, t, s], in0=bank[4 * t + n], scalar=stat[:, 7:8], in1=gfin[:, s],
                                               op0=ALU.mult, op1=ALU.mult)
            ins.then_inc(sem("out_ready"), 1)

        dve.wait_ge(sem("sims_ready"), PEER_H)
        route(0)
        route(1)
        dot_rows(0, 0)
        route(2)
        with link.loop(1, 8, ROUTE_PER) as g:
            dot_rows(g, 0)
            route(g + 2)
        dot_rows(8, 1)
        route(10)
        dve.wait_ge(sem("final_gain_landed"), 16)
        finish(0)
        with link.loop(9, 14, ROUTE_PER) as g:
            dot_rows(g, 1)
            route(g + 2)
        dot_rows(14, 1)
        dot_rows(15, 1)
        finish(1)

    ctx.close()


DSA_PER = 14
GLA_PER = 8
ROUTE_PER = 29

_INS = ['x', 'mem', 'positions', 'norm_mix_g', 'w_in', 'gla_gate_w2', 'gla_gate_b', 'gla_head_norm_g', 'w_proj_gla',
        'w_proj_dsa', 'w_out', 'norm_x_g', 'norm_mem_g', 'w_xq', 'w_xk', 'w_xv', 'w_xo', 'norm_ffn_g', 'peer_wq',
        'peer_sub_keys', 'peer_u', 'peer_v', 'norm_final_g']


def kernel(**inputs):
    import concourse.bacc as bacc
    from concourse.bass_utils import run_bass_kernel_spmd

    nc = bacc.Bacc("TRN2", target_bir_lowering=False, num_devices=1)
    arrays = {f"in_{n}": np.ascontiguousarray(inputs[n]) for n in _INS}
    arrays["in_consts"] = constants()
    args = {n[3:]: nc.dram_tensor(n, v.shape, mybir.dt.from_np(v.dtype), kind="ExternalInput").ap() for n, v in arrays.items()}
    args["out"] = nc.dram_tensor("out_0", (1, T, D), F32, kind="ExternalOutput").ap()
    hybrid_block(nc, args)
    r = run_bass_kernel_spmd(nc, [arrays], core_ids=[0])
    return r.results[0]["out_0"]
```

```python
from contextlib import ExitStack, contextmanager

import numpy as np

import concourse.bass as bass
from concourse import mybir

F32 = mybir.dt.float32
F32R = mybir.dt.float32r
I32 = mybir.dt.int32
U32 = mybir.dt.uint32
ALU = mybir.AluOpType
ACT = mybir.ActivationFunctionType
AX = mybir.AxisListType

P = 128
T = 256
TT = T // P
D = 2048
KT = D // P
CH = 256
UQ = 4
UK = KT // UQ
EPS = 1e-6

GLA_H, DK, DV, RANK = 4, 256, 512, 16
GATE_TEMP = 16.0
DSA_H, DH, IDX_H, IDX_D = 16, 128, 16, 64
TOPK = min(256, T // 4)
XH, XD = 4, D // 4
PEER_H, NKEYS, PTOP = 8, 128, 16
GROUPS = TT * PEER_H
RING = 8
BATCH = 4
VCOLS = D // 2
LATE = (GROUPS - 2, GROUPS - 1)
EARLY = LATE[0]
LATE_UNIT = 32
ALONE = 6
PLACES = 8
SPREAD = 16

COL = {}
_at = 0
for _name, _w in (("g_q", GLA_H * DK), ("g_k", GLA_H * DK), ("g_v", GLA_H * DV), ("g_r", GLA_H * DV), ("g_low", RANK),
                  ("d_q", DSA_H * DH), ("d_k", DH), ("d_v", DH), ("i_q", IDX_H * IDX_D), ("i_k", IDX_D), ("i_w", IDX_H),
                  ("gate_a", D), ("gate_b", D)):
    COL[_name] = _at
    _at += _w
IN_DIM = _at

IQ = 0
DQ = IQ + 2
GB = DQ + 4
GL = GB + 8
GA = GL + 12
XK = GA + 8
WO = XK + 4
XV = WO + 4
XQ = XV + 4
XO = XQ + 4
PQ = XO + 4
END = PQ + 4

LEVELS = (64, 32, 16, 8, 4, 2, 1)
C_IDENT = 0
C_MASK = P
C_COLS = C_MASK + P * len(LEVELS)
C_IOTA = C_COLS + 8
C_END = C_IOTA + NKEYS
INV_D, SGN_D, INV_I, SGN_I, EPSC = range(C_COLS, C_COLS + 5)

G_MIX, G_X, G_MEM, G_FFN, G_HEAD, G_BIAS, G_ROWS = 0, 16, 32, 48, 64, 80, 88

TWO_PI_1 = 6.28125
TWO_PI_2 = 0.00193500518798828125
TWO_PI_3 = 2 * np.pi - TWO_PI_1 - TWO_PI_2
ROUND = 1.5 * 2.0 ** 23
PI = 3.1415925
HIDDEN = -1.0e38
TAKEN = -3.0e38
NEG = -1.0e30


def constants():
    c = np.zeros((P, C_END), np.float32)
    c[:, C_IDENT:C_IDENT + P] = np.eye(P, dtype=np.float32)
    j, i = np.arange(P)[:, None], np.arange(P)[None, :]
    for n, m in enumerate(LEVELS):
        c[:, C_MASK + n * P:C_MASK + (n + 1) * P] = (j // (2 * m) == i // (2 * m)) & (j % (2 * m) < m) & (i % (2 * m) >= m)
    for d, inv, sgn in ((DH, INV_D, SGN_D), (IDX_D, INV_I, SGN_I)):
        freq = np.float32(10000.0) ** (-np.arange(0, d, 2, dtype=np.float32) / np.float32(d))
        k = np.arange(P) % d
        c[:, inv] = freq[k % (d // 2)]
        c[:, sgn] = np.where(k < d // 2, -1.0, 1.0)
    c[:, EPSC] = EPS
    c[:, C_IOTA:] = np.arange(NKEYS, dtype=np.float32)
    return c


class Chain:

    def __init__(self, eng, sem, apart):
        self.eng, self.sem, self.apart, self.base, self.n = eng, sem, apart, 0, 0

    def __call__(self, *steps):
        for ins in steps:
            ins.then_inc(self.sem, 1)
            self.n += 1
        self.apart(self.sem, self.base + self.n)

    @contextmanager
    def loop(self, lo, hi, per):
        start = self.base + self.n
        with self.eng.Fori(lo, hi) as i:
            self.base, self.n = i * per + (start - lo * per), 0
            yield i
            assert self.n == per, f"the body has {self.n} chained steps, not {per}"
        self.base, self.n = start + (hi - lo) * per, 0


class Apart:

    def __init__(self, eng, met):
        self.eng, self.met, self.value = eng, met, eng.alloc_register("wait_value")

    def __call__(self, sem, value):
        if isinstance(value, int):
            wait(self.eng, sem, value)
        else:
            self.eng.reg_mov(self.value, value)
            self.eng.wait_ge(self.met, 1)
            self.eng.wait_ge(sem, self.value)


def wait(eng, sem, value):
    if not isinstance(value, int) or value > 0:
        eng.wait_ge(sem, value)


def hybrid_block(nc, a):
    ctx = ExitStack()
    sems = {}

    def sem(name):
        if name not in sems:
            sems[name] = ctx.enter_context(nc.semaphore(name))
        return sems[name]

    base = (nc.sbuf_base + 63) // 64 * 64
    K = 1024

    def sb(name, shape, at, dt=F32):
        return nc.alloc_sbuf_tensor_at("b_" + name, [P] + list(shape), dt, offset=base + int(at))[:]

    RAW, HI, LO, ACTV, ATTN, HT, SCR, MRG, WRK, SML = (0, 32 * K, 48 * K, 64 * K, 96 * K, 128 * K, 144 * K, 160 * K,
                                                       176 * K, 192 * K)
    raw = sb("raw", [2 * UQ, UK, CH], RAW)
    w_hi = sb("w_hi", [UQ, UK, CH], HI, F32R)
    w_lo = sb("w_lo", [UQ, UK, CH], LO, F32R)
    act_hi = sb("act_hi", [KT, T], ACTV, F32R)
    act_lo = sb("act_lo", [KT, T], ACTV + 16 * K, F32R)
    att_hi = sb("att_hi", [KT, T], ATTN, F32R)
    att_lo = sb("att_lo", [KT, T], ATTN + 16 * K, F32R)
    hT = sb("hT", [KT, T], HT)
    scr = sb("scr", [KT, T], SCR)
    merged = sb("merged", [KT, T], MRG)
    xN = sb("xN", [TT, D], MRG)
    kcT = sb("kcT", [KT, T], MRG)
    vcN = sb("vcN", [TT, D], WRK)
    memN = sb("memN", [TT, D], SCR)
    memT = sb("memT", [KT, T], WRK)
    SMALLW = 3 * P + IDX_H + RANK
    ROWS = DH + IDX_H + RANK
    small_w = sb("small_w", [KT, SMALLW], ATTN)
    cos_d, sin_d, cos_i, sin_i = (sb(n, [T], WRK + k * K) for k, n in enumerate(("cos_d", "sin_d", "cos_i", "sin_i")))
    kiT = sb("kiT", [T], WRK + 4 * K)
    kdT = sb("kdT", [T], WRK + 5 * K)
    vdN = sb("vdN", [TT, DH], WRK + 6 * K)
    score = sb("score", [3 * P], WRK + 7 * K)
    sel_work = sb("sel_work", [3 * P], WRK + 8.5 * K)
    keep = sb("keep", [3 * P], WRK + 10 * K)
    relu = sb("relu", [2, 3 * P], WRK + 11.5 * K)
    idx_w = sb("idx_w", [TT, IDX_H], WRK + 14.5 * K)
    top8 = sb("top8", [8], WRK + 14.75 * K)
    pos_i = sb("pos_i", [T], WRK + 7 * K, I32)
    pos_f = sb("pos_f", [T], WRK + 8 * K)
    angle = sb("angle", [T], WRK + 9 * K)
    turns = sb("turns", [T], WRK + 10 * K)
    qbuf = sb("qbuf", [2, 2, T], SCR)
    swap = sb("swap", [2, T], SCR + 4 * K)
    rot = sb("rot", [2, T], SCR + 6 * K)
    probs = sb("probs", [4, 3, P], SCR + 8 * K)
    cum = sb("cum", [2 * GLA_H, T], WRK)
    attn = sb("attn", [3, P], WRK + 8 * K)
    decay = [sb(f"decay{n}", [2, T], WRK + (9.5 + 2 * n) * K) for n in range(2)]
    osq = sb("osq", [4, T], WRK + 9.5 * K)
    gz = sb("gz", [8, T], SCR)
    ge = sb("ge", [8, T], SCR + 8 * K)
    qg = sb("qg", [2, T], SCR)
    kg = sb("kg", [2, T], SCR + 2 * K)
    onorm = sb("onorm", [4, T], SCR)
    vg = sb("vg", [TT, DV], SCR + 4 * K)
    swish = sb("swish", [4, T], SCR + 8 * K)
    zlev = [sb("zlev0", [2, T], SCR + 12 * K), sb("zlev1", [2, T], SCR + 14 * K), sb("zlev2", [2, T], WRK + 13.5 * K)]
    qx = sb("qx", [2, 4, T], SCR)
    px = sb("px", [2, TT, T], SCR + 8 * K)
    pxT = sb("pxT", [2, TT, T], SCR + 12 * K)
    hN = sb("hN", [TT, D], WRK)
    xnN = sb("xnN", [TT, D], HT)
    skN = sb("skN", [2 * PEER_H, P], MRG)
    skT = sb("skT", [2 * PEER_H, P], MRG + 8 * K)
    qp = sb("qp", [2, 2, T], MRG)
    sims = sb("sims", [GROUPS, 2, NKEYS], SCR)
    R = MRG + 4 * K
    sc = sb("sc", [2, NKEYS], R)
    sc2 = sb("sc2", [2, NKEYS], R + K)
    cand = sb("cand", [PTOP, PTOP], R + 2 * K)
    cand2 = sb("cand2", [PTOP, PTOP], R + 3 * K)
    u_ring = sb("u_ring", [RING, D], ACTV)
    u_first = sb("u_first", [RING // 2, D], RAW)
    spread = sb("spread", [TT, NKEYS, P], RAW)
    late_row = [sb(f"late_row{n}", [D], RAW + n * 64 * K) for n in range(2)]
    late_sum = sb("late_sum", [D], RAW + 8 * K)
    row_hot = sb("row_hot", [RING, NKEYS], MRG)
    col_hot = sb("col_hot", [SPREAD, NKEYS], MRG + 8 * K)
    e_hi = sb("e_hi", [2, BATCH, T], MRG, F32R)
    e_lo = sb("e_lo", [2, BATCH, T], MRG + 8 * K, F32R)
    v_raw = [sb(f"v_raw{n}", [VCOLS], (HT if n < 2 else WRK + 4 * K) + n % 2 * 4 * K + n // 2 * 4 * K) for n in range(4)]
    v_hi = sb("v_hi", [2, VCOLS], SCR, F32R)
    v_lo = sb("v_lo", [2, VCOLS], SCR + 8 * K, F32R)
    gfin = sb("gfin", [D], HT)

    consts = sb("consts", [C_END], SML)
    s1 = SML + 4 * ((C_END + 7) // 8 * 8)
    ones = sb("ones", [T], s1)
    gains = sb("gains", [G_ROWS], s1 + K)
    g_low = sb("g_low", [T], s1 + K + 384)
    rstd = sb("rstd", [T], s1 + 2 * K + 384)
    masked = sb("masked", [TT, P], s1 + 3 * K + 384)
    sg = sb("sg", [2, 2, T], s1 + 4 * K + 384)
    low_rows = sb("low_rows", [TT, RANK], s1 + 5 * K + 384)
    gain_rows = sb("gain_rows", [P], s1 + 4 * K + 384)
    w2 = sb("w2", [GLA_H * DK], WRK + 11.5 * K)
    isel_all = sb("isel_all", [2, GROUPS * PTOP], s1 + 4 * K + 384)
    w_all = sb("w_all", [GROUPS * PTOP], s1 + 6 * K + 384)
    turned = sb("turned", [3, T], SML + 4 * C_MASK)
    onehot = sb("onehot", [PTOP, PTOP], s1)
    idx_all = sb("idx_all", [GROUPS * PTOP], s1 + K + 384, U32)
    gates_all = sb("gates_all", [GROUPS * PTOP], s1 + 2 * K + 384)
    s0 = s1 + 3 * K + 384
    tv = sb("tv", [2, PTOP], s0)
    ti = sb("ti", [2, PTOP], s0 + 128, U32)
    tif = sb("tif", [2, PTOP], s0 + 256)
    cv = sb("cv", [PTOP], s0 + 384)
    ci = sb("ci", [PTOP], s0 + 448, U32)
    cpart = sb("cpart", [2, PTOP], s0 + 512, U32)
    cpartf = sb("cpartf", [2, PTOP], s0 + 640)
    s2 = s1 + 8 * K + 384
    negmax = sb("negmax", [8], s2)
    psums = sb("psums", [8], s2 + 32)
    prec = sb("prec", [8], s2 + 64)
    gsum = sb("gsum", [8], s2 + 96)
    stat = sb("stat", [8], s2 + 128)
    egate = sb("egate", [PTOP], s2 + 160)
    dots = sb("dots", [PTOP], s2 + 224)
    gelu = sb("gelu", [PTOP], s2 + 288)
    stage_place = sb("stage_place", [3, SPREAD], s2 + 672)
    late_dots = sb("late_dots", [4], s2 + 864)
    stage_idx = sb("stage_idx", [4, PTOP], s2 + 416, U32)
    assert base + s2 + 880 <= nc.sbuf_usable_end

    ident = consts[:, C_IDENT:C_IDENT + P]

    def const(n):
        return consts[:, n:n + 1]

    def mask(n):
        return consts[:, C_MASK + n * P:C_MASK + (n + 1) * P]

    bank = [nc.alloc_psum_tensor(f"bank{n}", [P, 512], F32)[:] for n in range(8)]
    proj = [bank[c].rearrange("p (n t) -> p n t", n=2) for c in range(2)]

    w_landed = [sem(f"w_landed{s}") for s in range(2 * UQ)]
    w_high = sem("w_high")
    w_split = sem("w_split")
    units_used = sem("units_used")
    bank_free = [sem(f"bank_free{c}") for c in range(2)]

    def unit(p, c, q=0):
        return 8 * p + 4 * c + q

    def halves(x, m):
        return x.rearrange("p a (n s m) -> p (a n) s m", s=2, m=m)

    def load_pair(sp, apart, p, sources):
        for c, (w, col) in enumerate(sources):
            rows = w.rearrange("(q k p) n -> q p k n", q=UQ, p=P)
            for q in range(UQ):
                apart(w_split, unit(p, c, q) - 2 * UQ + 1)
                sp.dma_start(raw[:, UQ * c + q], rows[q][:, :, bass.ds(col, CH)]).then_inc(w_landed[UQ * c + q], 16)

    def split_high(act, p, c):
        for q in range(UQ):
            act.wait_ge(w_landed[UQ * c + q], p * 16 + 16)
            wait(act, units_used, unit(p, c, q) - UQ + 1)
            act.activation(w_hi[:, q], raw[:, UQ * c + q], ACT.Copy).then_inc(w_high, 1)

    def split_low(dve, p, c):
        for q in range(UQ):
            dve.wait_ge(w_high, unit(p, c, q) + 1)
            dve.tensor_tensor(w_lo[:, q], raw[:, UQ * c + q], w_hi[:, q].bitcast(F32), ALU.subtract).then_inc(w_split, 1)

    def multiply(pe, p, c, hi, lo, tokens_out=False, operand=None):
        wait(pe, bank_free[c], p)
        for q in range(UQ):
            pe.wait_ge(w_split, unit(p, c, q) + 1)
            if operand is not None:
                operand_ready(pe, operand, q + 1)
            for n in range(2):
                for k in range(UK):
                    kt = UK * q + k
                    for t, (x, w) in enumerate(((hi, w_hi), (lo, w_hi), (hi, w_lo))):
                        if tokens_out:
                            lhs, rhs = x[:, kt, n * P:(n + 1) * P], w[:, q, k, :]
                        else:
                            lhs, rhs = w[:, q, k, n * P:(n + 1) * P], x[:, kt, :]
                        mm = pe.matmul(proj[c][:, n], lhs, rhs, start=(q == 0 and n == 0 and k == 0 and t == 0),
                                       stop=(q == UQ - 1 and k == UK - 1 and t == 2), skip_group_check=True)
            mm.then_inc(units_used, 1)

    def multiplied(eng, p, c):
        eng.wait_ge(units_used, unit(p, c + 1))

    def evacuating(eng, split, p, evac, last=False):
        split(eng, p, 1)
        evac(p, 0)
        if not last:
            split(eng, p + 1, 0)
        evac(p, 1)

    def nothing(p, c):
        pass

    NORMS = {"x": (0, 0), "mem": (2, 2), "h2": (6, 2), "h3": (10, 2)}
    OPERANDS = ("x", "mem", "merged", "h2", "h3")
    BY_BOTH = ("x", "h3")
    LOW_BY_POOL = {"x": (3,), "mem": (0, 1, 2, 3), "merged": (3,), "h2": (0, 1, 2, 3), "h3": (3,)}

    def nth(names, tag, per=1):
        return list(names).index(tag) * per

    def squares(eng, tag, src, quarters, on_activation=True):
        for q in quarters:
            k = slice(4 * q, 4 * q + 4)
            if on_activation:
                eng.activation(scr[:, k], src[:, k], ACT.Square).then_inc(sem("squares_activation"), 1)
            else:
                eng.tensor_tensor(scr[:, k], src[:, k], src[:, k], ALU.mult).then_inc(sem("squares_vector"), 1)

    def sum_tiles(dve, tag):
        act_before, dve_before = NORMS[tag]
        dve.wait_ge(sem("squares_activation"), act_before + (2 if tag in BY_BOTH else 4))
        if tag in BY_BOTH:
            dve.wait_ge(sem("squares_vector"), dve_before + 2)
        dve.tensor_reduce(rstd, scr.rearrange("p k t -> p t k"), AX.X, ALU.add).then_inc(sem("tile_sums"), 1)

    def norm_sum(pe, tag):
        pe.wait_ge(sem("tile_sums"), nth(NORMS, tag) + 1)
        pe.matmul(bank[6][:, 0:T], ones[:, 0:P], rstd, start=True, stop=True).then_inc(sem("norm_sums"), 1)

    def norm_root(act, tag):
        act.wait_ge(sem("norm_sums"), nth(NORMS, tag) + 1)
        act.activation(rstd, bank[6][:, 0:T], ACT.Sqrt, scale=1.0 / D, bias=const(EPSC)).then_inc(sem("norm_root"), 1)

    def norm_scale(dve, link, tag, src, row, quarters=range(4)):
        for q in quarters:
            if q == 0:
                dve.wait_ge(sem("norm_root"), nth(NORMS, tag) + 1)
                link(dve.reciprocal(rstd, rstd))
            for k in range(4 * q, 4 * q + 4):
                ins = dve.scalar_tensor_tensor(out=scr[:, k], in0=src[:, k], scalar=gains[:, row + k:row + k + 1], in1=rstd,
                                               op0=ALU.mult, op1=ALU.mult)
            ins.then_inc(sem("normed"), 1)

    def normed(eng, tag, quarters=4):
        eng.wait_ge(sem("normed"), nth(NORMS, tag, 4) + quarters)

    def operand_high(act, tag, src, hi):
        for q in range(4):
            if tag in NORMS:
                normed(act, tag, q + 1)
            act.activation(hi[:, 4 * q:4 * q + 4], src[:, 4 * q:4 * q + 4], ACT.Copy).then_inc(sem("operand_high"), 1)

    def lows_before(tag, pool):
        return sum((q in by) == pool for t, by in LOW_BY_POOL.items() if OPERANDS.index(t) < OPERANDS.index(tag)
                   for q in range(4))

    def operand_low(eng, tag, src, hi, lo, pool=False, quarters=range(4)):
        for q in quarters:
            if (q in LOW_BY_POOL[tag]) == pool:
                eng.wait_ge(sem("operand_high"), nth(OPERANDS, tag, 4) + q + 1)
                s = slice(4 * q, 4 * q + 4)
                eng.tensor_tensor(lo[:, s], src[:, s], hi[:, s].bitcast(F32), ALU.subtract
                                  ).then_inc(sem("operand_low_pool" if pool else "operand_low"), 1)

    def operand_ready(eng, tag, quarters=4):
        for pool in (False, True):
            n = sum((q in LOW_BY_POOL[tag]) == pool for q in range(quarters))
            if n:
                eng.wait_ge(sem("operand_low_pool" if pool else "operand_low"), lows_before(tag, pool) + n)

    TURNED = ("x", "mem")

    def turn_in(pe, tag, src, steps=range(8)):
        before = nth(TURNED, tag, 8)
        for j in steps:
            wait(pe, sem("copied_in"), before + j - 3 if j > 3 else 0)
            for k in range(2):
                for t in range(TT):
                    mm = pe.transpose(bank[2 + j % 4][:, k * T + t * P:k * T + (t + 1) * P],
                                      src[:, t, (2 * j + k) * P:(2 * j + k + 1) * P], ident)
            mm.then_inc(sem("turned_in"), 1)

    def copy_in(act, tag, dst, steps=range(8)):
        before = nth(TURNED, tag, 8)
        for j in steps:
            act.wait_ge(sem("turned_in"), before + j + 1)
            act.activation(dst[:, 2 * j:2 * j + 2], bank[2 + j % 4].rearrange("p (k t) -> p k t", k=2),
                           ACT.Copy).then_inc(sem("copied_in"), 1)

    def row_tile(k, first=False):
        return u_first[:, k - RING // 2] if first and RING // 2 <= k < RING else u_ring[:, k % RING]

    def over(eng, lo, hi, body):
        if hi - lo == 1:
            body(lo)
        else:
            with eng.Fori(lo, hi) as i:
                body(i)

    FIRST_DQ, LAST_DQ = 2 * DQ, 2 * GB - 1

    def chunk_in(s, lo, hi):
        return not isinstance(s, int) or lo <= s <= hi

    u_landed = [sem(f"u_landed{s}") for s in range(RING)]
    v_landed = [sem(f"v_landed{s}") for s in range(4)]
    w_in = a["w_in"][0]

    def square(name):
        return a[name][0]

    block = ctx.enter_context(nc.Block())

    @block.sync
    def _(sp):
        apart = Apart(sp, w_split)
        for half in range(2):
            d = slice(half * D // 2, (half + 1) * D // 2)
            sp.dma_start(xN[:, :, d], a["x"][0, :, d].rearrange("(t p) d -> p t d", p=P)).then_inc(sem(f"x_landed{half}"), 16)
        sp.wait_ge(sem("x_landed1"), 16)
        for dst, name, w in ((0, "i_k", IDX_D), (IDX_D, "i_k", IDX_D), (P, "d_k", DH), (2 * P, "d_v", DH), (3 * P, "i_w", IDX_H),
                             (3 * P + IDX_H, "g_low", RANK)):
            sp.dma_start(small_w[:, :, dst:dst + w],
                         w_in[:, COL[name]:COL[name] + w].rearrange("(k p) n -> p k n", p=P)).then_inc(sem("small_landed"), 16)
        for i in range(2):
            load_pair(sp, apart, IQ + i, [(w_in, COL["i_q"] + (2 * i + c) * CH) for c in range(2)])

        def stream(first, lo, hi, w, col=0):
            with sp.Fori(lo, hi) as i:
                load_pair(sp, apart, first + i, [(w, i * 2 * CH + col + c * CH) for c in range(2)])

        def gated(first, gate, w):
            with sp.Fori(0, 4) as i:
                load_pair(sp, apart, i * 2 + first, [(w_in, i * 2 * CH + COL[gate] + c * CH) for c in range(2)])
                load_pair(sp, apart, i * 2 + first + 1, [(w, i * 2 * CH + c * CH) for c in range(2)])

        stream(DQ, 0, 4, w_in, COL["d_q"])
        gated(GB, "gate_b", square("w_proj_dsa"))
        with sp.Fori(0, GLA_H) as h:
            load_pair(sp, apart, h * 3 + GL, [(w_in, h * DK + COL[n]) for n in ("g_q", "g_k")])
            load_pair(sp, apart, h * 3 + GL + 1, [(w_in, h * DV + COL["g_v"] + c * CH) for c in range(2)])
            load_pair(sp, apart, h * 3 + GL + 2, [(w_in, h * DV + COL["g_r"] + c * CH) for c in range(2)])
        gated(GA, "gate_a", square("w_proj_gla"))
        for first, name in ((XK, "w_xk"), (WO, "w_out"), (XV, "w_xv"), (XQ, "w_xq"), (XO, "w_xo"), (PQ, "peer_wq")):
            stream(first, 0, 4, square(name))
        sp.wait_ge(sem("dotted"), PEER_H * PTOP)
        sp.wait_ge(sem("seeded"), 1)
        v_rows = a["peer_v"][0]

        def load_values(b, first=False):
            for n in range(4 * BATCH):
                if not (first and n < 4):
                    apart(sem("v_split"), b * 4 * BATCH + (n - 3))
                rows = v_rows[bass.ds(b * 2 * BATCH * P + n // 2 * P, P)]
                sp.dma_start(v_raw[n % 4], rows[:, n % 2 * VCOLS:(n % 2 + 1) * VCOLS]).then_inc(v_landed[n % 4], 16)

        load_values(0, first=True)
        with sp.Fori(1, NKEYS // (2 * BATCH)) as b:
            load_values(b)
        sp.wait_ge(sem("v_split"), 2 * NKEYS - 2)
        sp.dma_start(gfin, a["norm_final_g"].partition_broadcast(P)).then_inc(sem("final_gain_landed"), 16)
        for t in range(TT):
            for n in range(4):
                sp.wait_ge(sem("out_ready"), 4 * t + n + 1)
                sp.dma_start(a["out"][0, t * P:(t + 1) * P, n * 512:(n + 1) * 512], hN[:, t, n * 512:(n + 1) * 512]
                             ).then_inc(sem("out_stored"), 16)
        sp.wait_ge(sem("out_stored"), 16 * TT * 4)

    @block.gpsimd
    def _(pool):
        apart = Apart(pool, sem("keep_ready"))

        def drop_hidden(out, in_, fill, done):
            pool.affine_select(out=out[:, 0:P], in_=in_[:, 0:P], compare_op=ALU.is_ge, fill=fill, base=0,
                               pattern=[[-1, P]], channel_multiplier=1)
            pool.affine_select(out=out[:, P:3 * P], in_=in_[:, P:3 * P], compare_op=ALU.is_ge, fill=fill, base=P,
                               pattern=[[-1, T]], channel_multiplier=1).then_inc(done, 1)

        operand_low(pool, "x", scr, act_hi, act_lo, pool=True)
        pool.wait_ge(sem("idx_added"), IDX_H)
        drop_hidden(sel_work, score, HIDDEN, sem("hidden_dropped"))
        pool.wait_ge(sem("selected"), 1)
        drop_hidden(keep, score, 0.0, sem("keep_ready"))

        pool.wait_ge(sem("gla_operand"), GLA_H)
        pool.dma_start(memN, a["mem"][0].rearrange("(t p) d -> p t d", p=P)).then_inc(sem("mem_landed"), 16)
        operand_low(pool, "mem", scr, act_hi, act_lo, pool=True)
        operand_low(pool, "merged", merged, att_hi, att_lo, pool=True)
        operand_low(pool, "h2", scr, att_hi, att_lo, pool=True)
        pool.wait_ge(sem("cross_scored"), XH)
        pool.dma_start(skN, a["peer_sub_keys"][0].rearrange("h s n d -> n (h s) d")).then_inc(sem("keys_landed"), 16)
        operand_low(pool, "h3", scr, att_hi, att_lo, pool=True)
        normed(pool, "h3")
        pool.wait_ge(sem("h_rows"), 8)
        for t in range(TT):
            pool.dma_start(xnN[:, t], a["norm_ffn_g"][0].partition_broadcast(P)).then_inc(sem("ffn_gain_landed"), 16)

        u_rows = a["peer_u"][0]

        def gather_rows(g, slot, early=False, chunk=None):
            pool.wait_ge(sem("routed"), g + 1)
            if not early:
                apart(sem("dotted"), g * PTOP + (1 - RING))
            pool.tensor_copy(stage_idx[:, slot], idx_all[:, bass.ds(g * PTOP, PTOP)]).then_inc(sem("idx_staged"), 1)
            apart(sem("idx_staged"), g + 1)
            for k in range(PTOP):
                if early and k == 0:
                    pool.wait_ge(units_used, unit(PQ, 0))
                if early and k == RING // 2:
                    pool.wait_ge(w_split, unit(END, 0))
                if early and k == RING + RING // 2:
                    pool.wait_ge(units_used, unit(END, 0))
                if not early or k >= RING:
                    apart(sem("dotted"), g * PTOP + (k - RING + 1))
                pool.indirect_dma_start(row_tile(k, early), None, u_rows,
                                        bass.IndirectOffsetOnAxis(ap=stage_idx[:, slot, k:k + 1], axis=0)
                                        ).then_inc(u_landed[k % RING], 16)
                if chunk is not None and k % 4 == 3:
                    if k > PTOP // 2:
                        mark_places(chunk + 1, (chunk + 1) * SPREAD, part=k // 4 - 2)
                    elif not isinstance(g, int) or g > PEER_H:
                        mark_places(chunk, chunk * SPREAD, part=k // 4 + 2)

        def mark_places(c, before, count=SPREAD, part=None):
            if not part:
                if isinstance(c, int) and c % PEER_H == 0:
                    pool.wait_ge(sem("tables_turned"), c // PEER_H + 1)
                apart(sem("places_marked"), before)
                apart(sem("rows_marked"), before if count == SPREAD else ALONE * SPREAD)
                pool.tensor_copy(stage_place, turned[:, :, bass.ds(c * SPREAD, SPREAD)]).then_inc(sem("place_staged"), 1)
                apart(sem("place_staged"), c + 1)
            for k in range(count) if part is None else range(4 * part, 4 * part + 4):
                if not isinstance(c, int) or c > 0:
                    apart(sem("token_spread"), c * SPREAD + (k + 1 - SPREAD))
                pool.tensor_scalar(col_hot[:, k], consts[:, C_IOTA:], stage_place[:, 1, k:k + 1], None, ALU.is_equal
                                   ).then_inc(sem("places_marked"), 1)
                if count == SPREAD:
                    if not isinstance(c, int) or c > 0 or k >= RING:
                        apart(sem("token_spread"), c * SPREAD + (k + 1 - RING))
                    pool.tensor_scalar(row_hot[:, k % RING], consts[:, C_IOTA:], stage_place[:, 0, k:k + 1],
                                       stage_place[:, 2, k:k + 1], ALU.is_equal, ALU.mult).then_inc(sem("rows_marked"), 1)

        gather_rows(0, 0, early=True)
        pool.wait_ge(sem("sims_ready"), PEER_H)
        gather_rows(1, 1)
        with pool.Fori(1, 4) as i:
            for s in range(2):
                gather_rows(i * 2 + s, s)
        gather_rows(8, 0, chunk=-1)
        gather_rows(9, 1, chunk=0)
        with pool.Fori(0, 2) as i:
            for n in range(2):
                gather_rows(i * 2 + (10 + n), n, chunk=i * 2 + (1 + n))
        for part in (2, 3):
            mark_places(ALONE - 1, (ALONE - 1) * SPREAD, part=part)

        def marked(c):
            return c * PLACES + ALONE * (SPREAD - PLACES)

        pool.wait_ge(sem("routed"), GROUPS)
        for n, g in enumerate(LATE):
            pool.tensor_copy(stage_idx[:, 2 + n], idx_all[:, g * PTOP:(g + 1) * PTOP]).then_inc(sem("idx_staged"), 1)
        for c in range(ALONE, PEER_H + 1):
            mark_places(c, marked(c), PLACES)
        with pool.Fori(PEER_H + 1, GROUPS) as c:
            mark_places(c, marked(c), PLACES)

        def split_weights(b, slot):
            if b > 1:
                apart(sem("v_used"), (b - 1) * 2 * BATCH)
            w = spread[:, :, b * BATCH:(b + 1) * BATCH].rearrange("p a i t -> p i a t")
            hi, lo = (x[:, slot].rearrange("p i (a t) -> p i a t", a=TT) for x in (e_hi, e_lo))
            pool.tensor_copy(hi, w).then_inc(sem("e_high"), 1)
            apart(sem("e_high"), b)
            pool.tensor_tensor(lo, w, hi.bitcast(F32), ALU.subtract).then_inc(sem("e_split"), 1)

        pool.wait_ge(sem("spread_copied"), T // 4)
        first = LATE_UNIT // (2 * BATCH)
        for b in range(1, first + 1):
            split_weights(b, b % 2)
        pool.wait_ge(sem("first_split"), 1)
        pool.wait_ge(sem("e_split"), first - 1)
        pool.wait_ge(sem("idx_staged"), GROUPS)
        for phase in range(4):
            steps = sorted([(8 * j, "batch", first + 6 * phase + j + 1) for j in range(6)] +
                           [(3 * k - 5, "row", k) for k in range(PTOP)])
            for _, what, k in steps:
                if what == "batch":
                    split_weights(k, k % 2)
                else:
                    n = phase * PTOP + k
                    wait(pool, sem("late_used"), n - 1)
                    pool.indirect_dma_start(late_row[n % 2], None, (u_rows, a["peer_v"][0])[phase % 2],
                                            bass.IndirectOffsetOnAxis(ap=stage_idx[:, 2 + phase // 2, k:k + 1], axis=0)
                                            ).then_inc(sem(f"late_landed{n % 2}"), 16)
        for b in range(first + 25, NKEYS // BATCH):
            split_weights(b, b % 2)

    @block.scalar
    def _(act):
        act.dma_start(consts, a["consts"]).then_inc(sem("consts_landed"), 16)
        for dst, src in ((gain_rows[G_MIX:G_X], a["norm_mix_g"][0].rearrange("(k p) -> k p", p=P)),
                         (gain_rows[G_X:G_MEM], a["norm_x_g"][0].rearrange("(k p) -> k p", p=P)),
                         (gain_rows[G_MEM:G_FFN], a["norm_mem_g"][0].rearrange("(k p) -> k p", p=P)),
                         (gain_rows[G_FFN:G_HEAD], a["norm_ffn_g"][0].rearrange("(k p) -> k p", p=P)),
                         (gain_rows[G_HEAD:G_BIAS], a["gla_head_norm_g"][0].rearrange("h (k p) -> (h k) p", p=P)),
                         (gain_rows[G_BIAS:G_ROWS], a["gla_gate_b"][0].rearrange("(k p) -> k p", p=P)),
                         (pos_i, a["positions"][0].partition_broadcast(P))):
            act.dma_start(dst, src).then_inc(sem("gains_landed"), 16)
        copy_in(act, "x", hT)
        act.wait_ge(sem("copied_in"), 8)
        squares(act, "x", hT, (0, 2))
        act.wait_ge(sem("gains_turned"), 1)
        act.activation(gains, bank[7][:, 0:G_ROWS], ACT.Copy).then_inc(sem("gains_ready"), 1)
        norm_root(act, "x")
        split_high(act, 0, 0)
        operand_high(act, "x", scr, act_hi)
        for n, tab in enumerate((sin_d, cos_d, sin_i, cos_i)):
            act.wait_ge(sem("angles"), n + 1)
            act.activation(tab, tab, ACT.Sin).then_inc(sem("tables"), 1)

        def swap_halves(src, w, done):
            for s in range(0, P, w):
                o = s ^ w
                ins = act.activation(swap[s:s + w, 0:src.shape[1]], src[o:o + w], ACT.Copy)
            ins.then_inc(done, 1)

        act.wait_ge(sem("small_done"), 3)
        operand_ready(act, "x")
        swap_halves(bank[2][:, 0:T].unsqueeze(1), IDX_D // 2, sem("small_swapped"))
        act.wait_ge(sem("small_roped"), 1)
        swap_halves(bank[3][:, 0:T].unsqueeze(1), DH // 2, sem("small_swapped"))
        rows = bank[4][:, 0:TT * ROWS].rearrange("p (t d) -> p t d", t=TT)
        act.activation(vdN, rows[:, :, 0:DH], ACT.Copy)
        act.activation(idx_w, rows[:, :, DH:DH + IDX_H], ACT.Copy, scale=IDX_H ** -0.5)
        act.activation(low_rows, rows[:, :, DH + IDX_H:], ACT.Copy).then_inc(sem("small_copied"), 1)

        def index_relu(s):
            for h in range(4 * s, 4 * s + 4):
                act.wait_ge(sem("idx_scored"), h + 1)
                wait(act, sem("idx_added"), h - 1)
                act.activation(relu[:, h % 2], bank[2 + h % 4][:, 0:3 * P], ACT.Relu, scale=IDX_D ** -0.5
                               ).then_inc(sem("idx_relued"), 1)

        def dsa_exp(j, par):
            for hh in range(2):
                n = 2 * par + hh
                act.wait_ge(sem("dsa_max"), j * 2 + hh + 1)
                for t, (lo, hi) in enumerate(((0, 1), (1, 3))):
                    ins = act.activation(probs[:, n, lo:hi], probs[:, n, lo:hi], ACT.Exp,
                                         bias=negmax[:, 2 * n + t:2 * n + t + 1], accum_out=psums[:, 2 * n + t:2 * n + t + 1])
                ins.then_inc(sem("dsa_exp"), 1)

        def dsa_copy_turned(j, par):
            for hh in range(2):
                n = 2 * par + hh
                act.wait_ge(sem("dsa_turned"), j * 2 + hh + 1)
                act.activation(probs[:, n], bank[2 + n][:, 0:3 * P].rearrange("p (b t) -> p b t", b=3), ACT.Copy
                               ).then_inc(sem("dsa_probsT"), 1)

        def dsa_high(j):
            for hh in range(2):
                act.wait_ge(sem("dsa_out"), j * 2 + hh + 1)
                act.activation(att_hi[:, bass.ds(j * 2 + hh, 1)], bank[6 + hh][:, 0:T].unsqueeze(1), ACT.Copy
                               ).then_inc(sem("dsa_high"), 1)

        def dsa_behind(s, c):
            if chunk_in(s - 3, FIRST_DQ, LAST_DQ):
                dsa_high(s - (FIRST_DQ + 3))
            if chunk_in(s - 1, FIRST_DQ, LAST_DQ):
                dsa_exp(s - (FIRST_DQ + 1), 1 - c)
            if chunk_in(s - 2, FIRST_DQ, LAST_DQ):
                dsa_copy_turned(s - (FIRST_DQ + 2), c)

        def swap_queries(p, c):
            s = p * 2 + c
            multiplied(act, p, c)
            wait(act, sem("small_roped"), 2)
            wait(act, sem("roped"), s)
            swap_halves(proj[c], (IDX_D if chunk_in(s, 0, FIRST_DQ - 1) and isinstance(s, int) else DH) // 2, sem("swapped"))
            if isinstance(s, int) and 1 <= s <= FIRST_DQ:
                index_relu(s - 1)
            if isinstance(s, int) and s == 1:
                act.wait_ge(sem("low_turned"), 1)
                act.activation(g_low[0:RANK], bank[7][0:RANK, 0:T], ACT.Copy).then_inc(sem("low_copied"), 1)
            dsa_behind(s, c)

        for p in range(4):
            evacuating(act, split_high, p, swap_queries)
        act.wait_ge(sem("keep_ready"), 1)
        act.dma_start(w2[0:RANK], a["gla_gate_w2"][0]).then_inc(sem("w2_landed"), 16)
        with act.Fori(4, GB) as p:
            evacuating(act, split_high, p, swap_queries)

        def sigmoid_gate(p, c):
            multiplied(act, p, c)
            act.activation(sg[:, c], proj[c], ACT.Sigmoid).then_inc(bank_free[c], 1)

        def gate_step(first, gate_evac=sigmoid_gate):
            def step(i):
                evacuating(act, split_high, i * 2 + first, gate_evac)
                evacuating(act, split_high, i * 2 + first + 1, nothing)
            return step

        def sigmoid_and_attention(p, c):
            sigmoid_gate(p, c)
            dsa_behind(2 * p + c, c)
            if c:
                dsa_high(7)

        gate_step(GB, sigmoid_and_attention)(0)

        act.wait_ge(sem("gate_abs"), 1)
        act.activation(ge, ge, ACT.Exp, scale=-1.0).then_inc(sem("gate_exp"), 1)
        act.wait_ge(sem("gate_exp"), 1)
        act.activation(ge, ge, ACT.Ln, bias=1.0).then_inc(sem("gate_ln"), 1)
        with act.Fori(1, 4) as i:
            gate_step(GB)(i)
        act.wait_ge(sem("gates_summed"), 1)

        def gla_head(h):
            def level_decays(lo, hi):
                for lev in range(lo, hi):
                    m = P >> lev
                    e = halves(decay[lev % 2], m)
                    act.wait_ge(sem("gla_diff"), h * 8 + lev + 1)
                    act.activation(e[:, :, 0], e[:, :, 0], ACT.Exp, scale=-1.0 / GATE_TEMP)
                    act.activation(e[:, :, 1], e[:, :, 1], ACT.Exp, scale=1.0 / GATE_TEMP).then_inc(sem("gla_decay"), 1)

            def evac_qk(p, c):
                multiplied(act, p, c)
                if c == 0:
                    wait(act, sem("gla_operand"), h)
                act.activation((qg, kg)[c], proj[c], ACT.Copy, scale=(DK ** -0.5, 1.0)[c]).then_inc(bank_free[c], 1)

            def evac_v(p, c):
                multiplied(act, p, c)
                act.activation(vg[:, :, c * CH:(c + 1) * CH], proj[c], ACT.Copy).then_inc(bank_free[c], 1)

            def evac_r(p, c):
                multiplied(act, p, c)
                act.activation(swish[:, 2 * c:2 * c + 2], proj[c], ACT.Silu).then_inc(bank_free[c], 1)

            p = h * 3 + GL
            evacuating(act, split_high, p, evac_qk)
            level_decays(0, 3)
            split_high(act, p + 1, 1)
            evac_v(p + 1, 0)
            level_decays(3, 6)
            split_high(act, p + 2, 0)
            evac_v(p + 1, 1)
            level_decays(6, 8)
            evacuating(act, split_high, p + 2, evac_r)
            act.wait_ge(sem("gla_out"), h + 1)
            act.wait_ge(sem("gla_attn"), h + 1)
            for n in range(2):
                act.activation(osq[:, 2 * n:2 * n + 2], bank[6 + n].rearrange("p (e t) -> p e t", e=2), ACT.Square
                               ).then_inc(sem("gla_squares"), 1)
            act.wait_ge(sem("gla_sums"), h + 1)
            act.activation(rstd, bank[5][:, 0:T], ACT.Sqrt, scale=1.0 / DV, bias=const(EPSC)).then_inc(sem("gla_root"), 1)
            act.wait_ge(sem("gla_gated"), h + 1)
            act.activation(att_hi[:, bass.ds(h * 4, 4)], onorm, ACT.Copy).then_inc(sem("gla_high"), 1)

        gla_head(0)
        with act.Fori(1, GLA_H) as h:
            gla_head(h)

        gate_step(GA)(0)
        copy_in(act, "mem", memT, range(4))
        gate_step(GA)(1)
        copy_in(act, "mem", memT, range(4, 8))
        act.wait_ge(sem("copied_in"), 16)
        squares(act, "mem", memT, range(4))
        gate_step(GA)(2)

        def sigmoid_and_root(p, c):
            sigmoid_gate(p, c)
            if c == 0:
                norm_root(act, "mem")

        evacuating(act, split_high, GA + 6, sigmoid_and_root)
        split_high(act, GA + 7, 1)
        act.wait_ge(units_used, unit(GA + 7, 0))
        operand_high(act, "mem", scr, act_hi)
        split_high(act, XK, 0)
        act.wait_ge(units_used, unit(XK, 0))
        act.wait_ge(bank_free[1], XK)
        operand_high(act, "merged", merged, att_hi)
        operand_ready(act, "merged")

        def copy_out(dst, lead):
            def evac(p, c):
                multiplied(act, p, c)
                act.activation(dst(p - lead, c), proj[c], ACT.Copy).then_inc(bank_free[c], 1)
            return evac

        def run(first, lo, hi, evac):
            over(act, lo, hi, lambda i: evacuating(act, split_high, i + first, evac))

        def keys_at(i, c):
            return kcT[:, bass.ds(i * 4 + 2 * c, 2)]

        def values_at(i, c):
            return vcN[:, :, bass.ds(i * 2 * CH + c * CH, CH)]

        run(XK, 0, 4, copy_out(keys_at, XK))
        run(WO, 0, 4, nothing)
        act.wait_ge(bank_free[1], XV)
        squares(act, "h2", hT, range(4))
        run(XV, 0, 1, copy_out(values_at, XV))
        run(XV, 1, 2, copy_out(values_at, XV))
        norm_root(act, "h2")
        evacuating(act, split_high, XV + 2, copy_out(values_at, XV))
        operand_high(act, "h2", scr, att_hi)
        run(XV, 3, 4, copy_out(values_at, XV))
        operand_ready(act, "h2")

        def cross_exp(h):
            act.wait_ge(sem("cross_max"), h + 1)
            for t in range(TT):
                n = 2 * (h % 2) + t
                ins = act.activation(px[:, h % 2, t], bank[2 + h % 2][:, t * T:(t + 1) * T], ACT.Exp, scale=XD ** -0.5,
                                     bias=negmax[:, n:n + 1], accum_out=psums[:, n:n + 1])
            ins.then_inc(sem("cross_exp"), 1)

        def cross_copy_turned(h):
            act.wait_ge(sem("cross_turned"), h + 1)
            act.activation(pxT[:, h % 2], bank[4 + h % 2].rearrange("p (m t) -> p m t", m=2), ACT.Copy
                           ).then_inc(sem("cross_probsT"), 1)

        def cross_high(h):
            act.wait_ge(sem("cross_out"), h + 1)
            for n in range(2):
                ins = act.activation(act_hi[:, 4 * h + 2 * n:4 * h + 2 * n + 2], bank[6 + n].rearrange("p (e t) -> p e t", e=2),
                                     ACT.Copy)
            ins.then_inc(sem("cross_high"), 1)

        for h in range(XH):
            def evac(p, c, h=h):
                multiplied(act, p, c)
                wait(act, sem("cross_scored"), h - 1)
                act.activation(qx[:, h % 2, 2 * c:2 * c + 2], proj[c], ACT.Copy).then_inc(bank_free[c], 1)
                if c == 0:
                    if h >= 2:
                        cross_high(h - 2)
                    if h >= 1:
                        cross_exp(h - 1)
                elif h >= 1:
                    cross_copy_turned(h - 1)
            evacuating(act, split_high, XQ + h, evac)
        cross_exp(XH - 1)
        cross_high(XH - 2)
        cross_copy_turned(XH - 1)
        cross_high(XH - 1)

        run(XO, 0, 4, nothing)
        act.wait_ge(bank_free[1], PQ)
        squares(act, "h3", hT, (0, 2))
        for j in range(8):
            act.wait_ge(sem("rows_turned"), j + 1)
            act.activation(hN[:, j // 4, (j % 4) * 512:(j % 4 + 1) * 512], bank[2 + j % 4], ACT.Copy).then_inc(sem("h_rows"), 1)
        norm_root(act, "h3")
        operand_high(act, "h3", scr, att_hi)
        for n in range(4):
            act.wait_ge(sem("keys_turned"), n + 1)
            act.activation(skT[:, 4 * n:4 * n + 4], bank[2 + n].rearrange("p (g n) -> p g n", g=4), ACT.Copy
                           ).then_inc(sem("keys_ready"), 1)
        split_high(act, PQ, 1)
        operand_ready(act, "h3")
        for t in range(TT):
            act.wait_ge(sem("h_rows"), 8)
            act.activation(scr.rearrange("p k t -> p (k t)")[:, t * D:(t + 1) * D], hN[:, t], ACT.Square,
                           accum_out=gsum[:, t:t + 1]).then_inc(sem("row_squares"), 1)
        act.wait_ge(sem("row_squares"), 2)
        act.activation(stat[:, 0:2], gsum[:, 0:2], ACT.Sqrt, scale=1.0 / D, bias=const(EPSC)).then_inc(sem("row_root"), 1)

        def peer_pair(p, i, last=False):
            def evac(p, c):
                multiplied(act, p, c)
                wait(act, sem("peer_scored"), i * 2 - 2 + c + 1)
                act.activation(qp[:, c], proj[c], ACT.Copy).then_inc(bank_free[c], 1)
            if i > 0:
                split_high(act, p, 1)
            evac(p, 0)
            if not last:
                split_high(act, p + 1, 0)
            evac(p, 1)
            for c in range(2):
                act.wait_ge(sem("peer_scored"), i * 2 + c + 1)
                view = bank[2 + c].rearrange("p (s t n) -> p s t n", s=2, t=TT)
                for t in range(TT):
                    dst = sims[:, bass.ds(i * 2 + (t * PEER_H + c), 1)].rearrange("p g s n -> p (g s) n")
                    ins = act.activation(dst, view[:, :, t], ACT.Copy)
                ins.then_inc(sem("sims_ready"), 1)

        act.wait_ge(sem("keys_ready"), 4)
        def gate_exp(g):
            act.wait_ge(sem("cands_ready"), g + 1)
            act.activation(egate, cv, ACT.Exp, bias=stat[:, 4:5], accum_out=stat[:, 5:6]).then_inc(sem("gate_exped"), 1)

        def spread_out(c, t):
            for m in range(SPREAD // 4):
                act.wait_ge(sem("token_spread"), c * SPREAD + 4 * m + 4)
                act.activation(spread[:, t, :, bass.ds(c * SPREAD + (4 * m - t * P), 4)].rearrange("p i t -> p t i"),
                               bank[m % 2].rearrange("p (t i) -> p t i", t=4),
                               ACT.Copy).then_inc(sem("spread_copied"), 1)

        def turned_tables(t):
            act.wait_ge(sem("tables_in_bank"), t + 1)
            act.activation(turned[:, :, t * P:(t + 1) * P], bank[0][:, 0:3 * P].rearrange("p (n t) -> p n t", n=3), ACT.Copy
                           ).then_inc(sem("tables_turned"), 1)

        def expert_gelu(g):
            act.wait_ge(sem("dotted"), g * PTOP + PTOP)
            wait(act, sem("weights_ready"), g)
            act.activation(gelu, dots, ACT.Gelu_apprx_tanh).then_inc(sem("gelu_ready"), 1)

        def values_high(at, steps, first=False):
            for n in steps:
                act.wait_ge(v_landed[n % 4], at * 16 + (n // 4 + 1) * 16)
                if not (first and n < 2):
                    act.wait_ge(sem("v_high_used"), at * 4 + (n - 1))
                act.activation(v_hi[:, n % 2], v_raw[n % 4], ACT.Copy).then_inc(sem("v_high"), 1)

        peer_pair(PQ, 0)
        peer_pair(PQ + 1, 1)
        gate_exp(0)
        peer_pair(PQ + 2, 2)
        gate_exp(1)
        peer_pair(PQ + 3, 3, last=True)
        expert_gelu(0)
        gate_exp(2)
        gate_exp(3)
        with act.Fori(1, 8) as g:
            expert_gelu(g)
            gate_exp(g + 3)
        turned_tables(0)
        with act.Fori(8, EARLY - 1) as g:
            expert_gelu(g)
            gate_exp(g + 3)
            spread_out(g - 8, 0)
        expert_gelu(EARLY - 1)
        spread_out(EARLY - 1 - 8, 0)
        for c in range(ALONE, PEER_H):
            spread_out(c, 0)
        turned_tables(1)
        with act.Fori(8, GROUPS - 1) as c:
            spread_out(c, 1)
        values_high(0, range(2), first=True)
        spread_out(GROUPS - 1, 1)
        act.wait_ge(sem("spread_copied"), T // 4)
        act.activation(e_hi[:, 0].rearrange("p i (a t) -> p i a t", a=TT),
                       spread[:, :, 0:BATCH].rearrange("p a i t -> p i a t"), ACT.Copy).then_inc(sem("first_high"), 1)
        values_high(0, range(2, 16), first=True)
        values_high(4, range(16))
        for phase in range(4):
            with act.Fori(0, 4) as i:
                values_high(i * 3 + (LATE_UNIT // 4 + 12 * phase), range(12))
            if phase % 2 == 0:
                act.wait_ge(sem("late_dots"), 2 * phase + 4)
                act.activation(gelu, dots, ACT.Gelu_apprx_tanh).then_inc(sem("gelu_ready"), 1)
        with act.Fori(14, 16) as b:
            values_high(b * 4, range(16))

        for n in (0, 1, 4, 5, 2, 3, 6):
            act.wait_ge(sem("v_used"), 2 * NKEYS - 1 + n % 4 // 2)
            ins = act.activation(hN[:, n // 4, n % 4 * 512:(n % 4 + 1) * 512], bank[n], ACT.Square, accum_out=gsum[:, n:n + 1])
        ins.then_inc(sem("out_squares"), 1)
        act.wait_ge(sem("out_summed"), 1)
        act.activation(stat[:, 6:8], stat[:, 6:8], ACT.Sqrt, scale=1.0 / D, bias=const(EPSC)).then_inc(sem("out_root"), 1)

    @block.tensor
    def _(pe):
        pe.wait_ge(sem("consts_landed"), 16)
        for half in range(2):
            pe.wait_ge(sem(f"x_landed{half}"), 16)
            turn_in(pe, "x", xN, range(4 * half, 4 * half + 4))
        pe.wait_ge(sem("gains_landed"), 16 * 7)
        pe.transpose(bank[7][:, 0:G_ROWS], gain_rows[0:G_ROWS], ident[0:G_ROWS, 0:G_ROWS]).then_inc(sem("gains_turned"), 1)
        pe.wait_ge(sem("ones_ready"), 1)
        norm_sum(pe, "x")

        pe.wait_ge(sem("small_landed"), 16 * 6)
        pe.wait_ge(sem("copied_in"), 8)
        pe.wait_ge(sem("gains_ready"), 1)

        def small(out, lhs, rhs):
            for k in range(KT):
                normed(pe, "x", k // 4 + 1)
                mm = pe.matmul(out, lhs(k), rhs(k), start=(k == 0), stop=(k == KT - 1))
            return mm

        small(bank[2][:, 0:T], lambda k: small_w[:, k, 0:P], lambda k: scr[:, k]).then_inc(sem("small_done"), 1)
        small(bank[3][:, 0:T], lambda k: small_w[:, k, P:2 * P], lambda k: scr[:, k]).then_inc(sem("small_done"), 1)
        for t in range(TT):
            mm = small(bank[4][:, t * ROWS:(t + 1) * ROWS], lambda k: scr[:, k, t * P:(t + 1) * P],
                       lambda k: small_w[:, k, 2 * P:])
        mm.then_inc(sem("small_done"), 1)

        operand_ready(pe, "x")
        def index_scores(s):
            if s == 0:
                pe.wait_ge(sem("small_roped"), 2)
                pe.wait_ge(sem("small_copied"), 1)
                for t in range(TT):
                    mm = pe.transpose(bank[7][0:RANK, t * P:(t + 1) * P], low_rows[:, t], ident)
                mm.then_inc(sem("low_turned"), 1)
            pe.wait_ge(sem("roped"), s + 1)
            for h in range(4 * s, 4 * s + 4):
                wait(pe, sem("idx_relued"), h - 3)
                c, n, x = s % 2, h // 2 % 2, slice(IDX_D * (h % 2), IDX_D * (h % 2 + 1))
                b = bank[2 + h % 4]
                pe.matmul(b[:, 0:P], qbuf[x, c, n, 0:P], kiT[x, 0:P], start=True, stop=True)
                pe.matmul(b[:, P:3 * P], qbuf[x, c, n, P:T], kiT[x], start=True, stop=True).then_inc(sem("idx_scored"), 1)

        def dsa_logits(j, par):
            if isinstance(j, int) and j < 2:
                pe.wait_ge(sem("low_copied"), 1)
                pe.wait_ge(sem("idx_relued"), IDX_H)
            pe.wait_ge(sem("roped"), j + (FIRST_DQ + 1))
            for hh in range(2):
                q, b = qbuf[:, par, hh], bank[2 + 2 * par + hh]
                pe.matmul(b[:, 0:P], q[:, 0:P], kdT[:, 0:P], start=True, stop=True)
                pe.matmul(b[:, P:3 * P], q[:, P:T], kdT, start=True, stop=True).then_inc(sem("dsa_logits"), 1)

        def dsa_turn(j, par):
            for hh in range(2):
                n = 2 * par + hh
                pe.wait_ge(sem("dsa_probs"), j * 2 + hh + 1)
                for b in range(3):
                    mm = pe.transpose(bank[2 + n][:, b * P:(b + 1) * P], probs[:, n, b], ident)
                mm.then_inc(sem("dsa_turned"), 1)

        def dsa_values(j, par):
            for hh in range(2):
                n, b = 2 * par + hh, bank[6 + hh]
                pe.wait_ge(sem("dsa_probsT"), j * 2 + hh + 1)
                wait(pe, sem("dsa_operand"), j * 2 + hh - 1)
                pe.matmul(b[:, 0:T], vdN[:, 0], probs[:, n, 0:2], start=True, stop=False, skip_group_check=True)
                pe.matmul(b[:, P:T], vdN[:, 1], probs[:, n, 2], start=False, stop=True, skip_group_check=True
                          ).then_inc(sem("dsa_out"), 1)

        def mix(p, c):
            s = p * 2 + c
            multiply(pe, p, c, act_hi, act_lo)
            if isinstance(s, int) and 1 <= s <= FIRST_DQ:
                index_scores(s - 1)
            if chunk_in(s - 3, FIRST_DQ, LAST_DQ):
                dsa_values(s - (FIRST_DQ + 3), 1 - c)
            if chunk_in(s - 1, FIRST_DQ, LAST_DQ):
                dsa_logits(s - (FIRST_DQ + 1), 1 - c)
            if chunk_in(s - 2, FIRST_DQ, LAST_DQ):
                dsa_turn(s - (FIRST_DQ + 2), c)

        for p in range(4):
            for c in range(2):
                mix(p, c)
        with pe.Fori(4, GB) as p:
            for c in range(2):
                mix(p, c)
        for c in range(2):
            mix(GB, c)
        dsa_values(7, 1)
        pe.wait_ge(sem("dsa_operand"), DSA_H)

        def project(p, c):
            multiply(pe, p, c, att_hi, att_lo)

        def gated(first, lo, hi):
            def step(i):
                for c in range(2):
                    multiply(pe, i * 2 + first, c, act_hi, act_lo)
                for c in range(2):
                    project(i * 2 + first + 1, c)
            over(pe, lo, hi, step)

        pe.wait_ge(sem("w2_landed"), 16)
        for n in range(8):
            mm = pe.matmul(bank[2 + n // 2][:, (n % 2) * T:(n % 2 + 1) * T], w2[0:RANK, n * P:(n + 1) * P], g_low[0:RANK],
                           start=True, stop=True)
        mm.then_inc(sem("gate_logits"), 1)
        for c in range(2):
            project(GB + 1, c)
        gated(GB, 1, 4)
        pe.wait_ge(sem("gate_biased"), 1)
        def gla_head(h):
            def scores(lo, hi):
                for lev in range(lo, hi):
                    b = bank[2 + lev % 3]
                    if lev < 8:
                        pe.wait_ge(sem("gla_z"), h * 8 + lev + 1)
                    wait(pe, sem("gla_added"), h * 9 + lev - 2)
                    z = zlev[lev % 3] if lev < 8 else None
                    for blk in range(1 if lev == 0 else 2):
                        s = slice(blk * P, (blk + 1) * P)
                        for d in range(2):
                            lhs, rhs = (kg[:, d, s], qg[:, d, s]) if lev == 8 else (
                                z[:, d, s], z[:, d, P:T] if lev == 0 else z[:, d, s])
                            mm = pe.matmul(b[:, s], lhs, rhs, start=(d == 0), stop=(d == 1))
                    mm.then_inc(sem("gla_scored"), 1)

            p = h * 3 + GL
            multiply(pe, p, 0, act_hi, act_lo)
            multiply(pe, p, 1, act_hi, act_lo)
            multiply(pe, p + 1, 0, act_hi, act_lo, tokens_out=True)
            scores(0, 3)
            multiply(pe, p + 1, 1, act_hi, act_lo, tokens_out=True)
            scores(3, 6)
            multiply(pe, p + 2, 0, act_hi, act_lo)
            scores(6, 9)
            multiply(pe, p + 2, 1, act_hi, act_lo)
            pe.wait_ge(sem("gla_attn"), h + 1)
            wait(pe, sem("gla_operand"), h)
            for e in range(4):
                b, o = bank[6 + e // 2], (e % 2) * T
                pe.matmul(b[:, o:o + T], vg[:, 0, e * P:(e + 1) * P], attn[:, 0:2], start=True, stop=False,
                          skip_group_check=True)
                mm = pe.matmul(b[:, o + P:o + T], vg[:, 1, e * P:(e + 1) * P], attn[:, 2], start=False, stop=True,
                               skip_group_check=True)
            mm.then_inc(sem("gla_out"), 1)
            for e in range(4):
                pe.wait_ge(sem("gla_squares"), h * 2 + e // 2 + 1)
                mm = pe.matmul(bank[5][:, 0:T], ones[:, 0:P], osq[:, e], start=(e == 0), stop=(e == 3))
            mm.then_inc(sem("gla_sums"), 1)

        gla_head(0)
        with pe.Fori(1, GLA_H) as h:
            gla_head(h)

        for c in range(2):
            multiply(pe, GA, c, act_hi, act_lo)
        pe.wait_ge(sem("gla_operand"), GLA_H)
        for c in range(2):
            project(GA + 1, c)
        pe.wait_ge(sem("mem_landed"), 16)
        turn_in(pe, "mem", memN, range(4))
        gated(GA, 1, 2)
        turn_in(pe, "mem", memN, range(4, 8))
        gated(GA, 2, 3)
        multiply(pe, GA + 6, 0, act_hi, act_lo)
        norm_sum(pe, "mem")
        multiply(pe, GA + 6, 1, act_hi, act_lo)
        for c in range(2):
            project(GA + 7, c)

        def run(first, lo, hi, hi_op, lo_op, tokens_out=False):
            def step(i):
                for c in range(2):
                    multiply(pe, i + first, c, hi_op, lo_op, tokens_out)
            over(pe, lo, hi, step)

        operand_ready(pe, "mem")
        run(XK, 0, 4, act_hi, act_lo)
        operand_ready(pe, "merged")
        run(WO, 0, 4, att_hi, att_lo)
        run(XV, 0, 1, act_hi, act_lo, True)
        multiply(pe, XV + 1, 0, act_hi, act_lo, True)
        norm_sum(pe, "h2")
        multiply(pe, XV + 1, 1, act_hi, act_lo, True)
        run(XV, 2, 4, act_hi, act_lo, True)

        def cross_logits(h):
            pe.wait_ge(bank_free[1], XQ + h + 1)
            for t in range(TT):
                for k in range(4):
                    mm = pe.matmul(bank[2 + h % 2][:, t * T:(t + 1) * T], qx[:, h % 2, k, t * P:(t + 1) * P], kcT[:, 4 * h + k],
                                   start=(k == 0), stop=(k == 3))
            mm.then_inc(sem("cross_scored"), 1)

        def cross_turn(h):
            pe.wait_ge(sem("cross_probs"), h + 1)
            for m in range(2):
                for t in range(TT):
                    mm = pe.transpose(bank[4 + h % 2][:, m * T + t * P:m * T + (t + 1) * P], px[:, h % 2, t, m * P:(m + 1) * P],
                                      ident)
            mm.then_inc(sem("cross_turned"), 1)

        def cross_values(h):
            pe.wait_ge(sem("cross_probsT"), h + 1)
            wait(pe, sem("cross_operand"), h)
            for e in range(4):
                for m in range(2):
                    o = h * XD + e * P
                    mm = pe.matmul(bank[6 + e // 2][:, (e % 2) * T:(e % 2 + 1) * T], vcN[:, m, o:o + P], pxT[:, h % 2, m],
                                   start=(m == 0), stop=(m == 1))
            mm.then_inc(sem("cross_out"), 1)

        operand_ready(pe, "h2")
        for h in range(XH):
            multiply(pe, XQ + h, 0, att_hi, att_lo)
            if h >= 2:
                cross_values(h - 2)
            if h >= 1:
                cross_logits(h - 1)
            multiply(pe, XQ + h, 1, att_hi, att_lo)
            if h >= 1:
                cross_turn(h - 1)
        cross_logits(XH - 1)
        cross_values(XH - 2)
        cross_turn(XH - 1)
        cross_values(XH - 1)

        pe.wait_ge(sem("cross_operand"), XH)
        run(XO, 0, 4, act_hi, act_lo)
        pe.wait_ge(bank_free[1], PQ)
        pe.wait_ge(sem("keys_landed"), 16)
        def turn_rows(steps):
            for j in steps:
                if j >= 4:
                    pe.wait_ge(sem("h_rows"), j - 3)
                t = j // 4
                for k in range(4):
                    mm = pe.transpose(bank[2 + j % 4][:, k * P:(k + 1) * P], hT[:, (j % 4) * 4 + k, t * P:(t + 1) * P], ident)
                mm.then_inc(sem("rows_turned"), 1)

        turn_rows(range(8))
        norm_sum(pe, "h3")
        for g in range(2 * PEER_H):
            if g % 4 == 0:
                pe.wait_ge(sem("h_rows"), 5 + g // 4)
            mm = pe.transpose(bank[2 + g // 4][:, (g % 4) * P:(g % 4 + 1) * P], skN[:, g], ident)
            if g % 4 == 3:
                mm.then_inc(sem("keys_turned"), 1)
        def peer_pair(i):
            for c in range(2):
                multiply(pe, i + PQ, c, att_hi, att_lo, operand="h3" if isinstance(i, int) else None)
            if isinstance(i, int):
                pe.wait_ge(sem("keys_ready"), 4)
            for c in range(2):
                pe.wait_ge(bank_free[c], i + PQ + 1)
                wait(pe, sem("sims_ready"), i * 2 + c - 1)
                for s in range(2):
                    for t in range(TT):
                        o = (s * TT + t) * NKEYS
                        mm = pe.matmul(bank[2 + c][:, o:o + NKEYS], qp[:, c, s, t * P:(t + 1) * P],
                                       skT[:, bass.ds(i * 4 + 2 * c + s, 1)].rearrange("p g n -> p (g n)"), start=True, stop=True)
                mm.then_inc(sem("peer_scored"), 1)

        peer_pair(0)
        with pe.Fori(1, 4) as i:
            peer_pair(i)

        def turn_tables(t):
            pe.wait_ge(sem("weights_ready"), min((t + 1) * PEER_H, EARLY))
            wait(pe, sem("spread_copied"), t * P // 4)
            for n, src in enumerate((isel_all[:, 0], isel_all[:, 1], w_all)):
                mm = pe.transpose(bank[0][:, n * P:(n + 1) * P], src[:, t * P:(t + 1) * P], ident)
            mm.then_inc(sem("tables_in_bank"), 1)
            pe.wait_ge(sem("tables_turned"), t + 1)

        def spread_weights(c, first=False, shared=False):
            for k in range(SPREAD):
                if k % 4 == 0 and not (first and k < 8):
                    pe.wait_ge(sem("spread_copied"), c * (SPREAD // 4) + (k // 4 - 1))
                if not shared:
                    pe.wait_ge(sem("places_marked"), c * SPREAD + k + 1)
                elif k < PLACES:
                    pe.wait_ge(sem("places_marked"), c * PLACES + (ALONE * (SPREAD - PLACES) + k + 1))
                elif k % 4 == 0:
                    pe.wait_ge(sem("more_places"), c * ((SPREAD - PLACES) // 4) + ((k - PLACES) // 4 + 1 - ALONE * (SPREAD - PLACES) // 4))
                if shared:
                    pe.wait_ge(sem("rows_ready"), c * SPREAD + (k + 1 - ALONE * SPREAD))
                else:
                    pe.wait_ge(sem("rows_marked"), c * SPREAD + k + 1)
                pe.matmul(bank[k // 4 % 2][:, k % 4 * P:(k % 4 + 1) * P], col_hot[:, k], row_hot[:, k % RING], start=True,
                          stop=True).then_inc(sem("token_spread"), 1)

        def seed(banks):
            for n in banks:
                mm = pe.matmul(bank[n], ident, hN[:, n // 4, n % 4 * 512:(n % 4 + 1) * 512], start=True, stop=False,
                               skip_group_check=True)
            return mm

        def values(b, first=False, last=False):
            for n in range(4 * BATCH):
                if first and n == 0:
                    pe.wait_ge(sem("first_split"), 1)
                elif n % (2 * BATCH) == 0:
                    pe.wait_ge(sem("e_split"), b * 2 + n // (2 * BATCH))
                pe.wait_ge(sem("v_split"), b * 4 * BATCH + n + 1)
                slot, i, v = n // (2 * BATCH), n // 2 % BATCH, n % 2
                for parts, x, done in (((e_hi, e_lo), v_hi, "v_high_used"), ((e_hi,), v_lo, "v_used")):
                    for t in range(TT):
                        for e in parts:
                            for m in range(2):
                                mm = pe.matmul(bank[4 * t + 2 * v + m], e[:, slot, i, t * P:(t + 1) * P],
                                               x[:, v, m * 512:(m + 1) * 512], start=False,
                                               stop=(last and n >= 4 * BATCH - 2 and x is v_lo), skip_group_check=True)
                    mm.then_inc(sem(done), 1)

        pe.wait_ge(sem("sims_ready"), PEER_H)
        seed(range(2, 8)).then_inc(sem("seeded"), 1)
        turn_tables(0)
        spread_weights(0, first=True)
        with pe.Fori(1, ALONE) as c:
            spread_weights(c)
        with pe.Fori(ALONE, PEER_H) as c:
            spread_weights(c, shared=True)
        turn_tables(1)
        with pe.Fori(8, GROUPS) as c:
            spread_weights(c, shared=True)
        pe.wait_ge(sem("spread_copied"), T // 4)
        seed(range(2))
        values(0, first=True)
        with pe.Fori(1, NKEYS // (2 * BATCH) - 1) as b:
            values(b)
        pe.wait_ge(sem("late_used"), 4 * PTOP)
        for n in range(4):
            pe.matmul(bank[4 + n], ident, late_sum[:, n * 512:(n + 1) * 512], start=False, stop=False, skip_group_check=True)
        values(NKEYS // (2 * BATCH) - 1, last=True)

    @block.vector
    def _(dve):
        link = Chain(dve, sem("vector_step"), Apart(dve, sem("ones_ready")))
        dve.memset(ones, 1.0).then_inc(sem("ones_ready"), 1)

        dve.wait_ge(sem("copied_in"), 8)
        squares(dve, "x", hT, (1, 3), on_activation=False)
        sum_tiles(dve, "x")
        dve.wait_ge(sem("gains_ready"), 1)
        norm_scale(dve, link, "x", hT, G_MIX)
        operand_low(dve, "x", scr, act_hi, act_lo)
        split_low(dve, 0, 0)

        dve.wait_ge(sem("gains_landed"), 16 * 7)
        link(dve.tensor_copy(pos_f, pos_i))
        for inv, sin_t, cos_t in ((INV_D, sin_d, cos_d), (INV_I, sin_i, cos_i)):
            link(dve.tensor_scalar(angle, pos_f, const(inv), None, ALU.mult))
            for tab, shift in ((sin_t, 0.0), (cos_t, 0.25)):
                link(dve.tensor_scalar(turns, angle, 1.0 / (2 * np.pi), shift, ALU.mult, ALU.add))
                link(dve.tensor_scalar(turns, turns, ROUND, None, ALU.add))
                link(dve.tensor_scalar(turns, turns, ROUND, None, ALU.subtract))
                link(dve.scalar_tensor_tensor(out=tab, in0=turns, scalar=-TWO_PI_1, in1=angle, op0=ALU.mult, op1=ALU.add))
                link(dve.scalar_tensor_tensor(out=tab, in0=turns, scalar=-TWO_PI_2, in1=tab, op0=ALU.mult, op1=ALU.add))
                link(dve.scalar_tensor_tensor(out=tab, in0=turns, scalar=-TWO_PI_3, in1=tab, op0=ALU.mult, op1=ALU.add))
                link(dve.tensor_scalar(tab, tab, shift * 2 * np.pi, PI, ALU.add, ALU.min))
                dve.tensor_scalar(tab, tab, -PI, None, ALU.max).then_inc(sem("angles"), 1)
        dve.wait_ge(sem("tables"), 4)
        for tab, sgn in ((sin_d, SGN_D), (sin_i, SGN_I)):
            link(dve.tensor_scalar(tab, tab, const(sgn), None, ALU.mult))

        def rope(src, n, cos_t, sin_t, out, done, bank_done=None):
            wide = [P, n, T]
            ins = dve.tensor_tensor(rot[:, 0:n], src, cos_t.unsqueeze(1).broadcast_to(wide), ALU.mult)
            if bank_done is not None:
                ins.then_inc(bank_done, 1)
            link(dve.tensor_tensor(swap[:, 0:n], swap[:, 0:n], sin_t.unsqueeze(1).broadcast_to(wide), ALU.mult))
            dve.tensor_tensor(out, rot[:, 0:n], swap[:, 0:n], ALU.add).then_inc(done, 1)

        dve.wait_ge(sem("small_swapped"), 1)
        rope(bank[2][:, 0:T].unsqueeze(1), 1, cos_i, sin_i, kiT.unsqueeze(1), sem("small_roped"))
        dve.wait_ge(sem("small_swapped"), 2)
        rope(bank[3][:, 0:T].unsqueeze(1), 1, cos_d, sin_d, kdT.unsqueeze(1), sem("small_roped"))

        def index_add(s):
            if s == 0:
                dve.wait_ge(sem("small_copied"), 1)
            for h in range(4 * s, 4 * s + 4):
                dve.wait_ge(sem("idx_relued"), h + 1)
                wait(dve, sem("idx_added"), h)
                for t, (lo, hi) in enumerate(((0, P), (P, 3 * P))):
                    w = idx_w[:, t, h:h + 1]
                    if h == 0:
                        ins = dve.tensor_scalar(score[:, lo:hi], relu[:, 0, lo:hi], w, None, ALU.mult)
                    else:
                        ins = dve.scalar_tensor_tensor(out=score[:, lo:hi], in0=relu[:, h % 2, lo:hi], scalar=w,
                                                       in1=score[:, lo:hi], op0=ALU.mult, op1=ALU.add)
                ins.then_inc(sem("idx_added"), 1)

        def select():
            dve.wait_ge(sem("hidden_dropped"), 1)
            for lo, hi in ((0, P), (P, 3 * P)):
                if lo == P:
                    split_low(dve, DQ + 1, 0)
                for _ in range(TOPK // 8):
                    link(dve.max(top8, sel_work[:, lo:hi]))
                    link(dve.match_replace(sel_work[:, lo:hi], top8, sel_work[:, lo:hi], TAKEN))
            dve.tensor_scalar(score, sel_work, 2 * HIDDEN, None, ALU.is_le).then_inc(sem("selected"), 1)

        def dsa_softmax(j, par):
            if isinstance(j, int) and j == 0:
                dve.wait_ge(sem("keep_ready"), 1)
                link(dve.tensor_scalar(keep, keep, 1.0, -NEG, ALU.subtract, ALU.mult))
            for hh in range(2):
                n = 2 * par + hh
                dve.wait_ge(sem("dsa_logits"), j * 2 + hh + 1)
                link(dve.scalar_tensor_tensor(out=probs[:, n].rearrange("p b k -> p (b k)"), in0=bank[2 + n][:, 0:3 * P],
                                              scalar=DH ** -0.5, in1=keep, op0=ALU.mult, op1=ALU.add))
                for t, (lo, hi) in enumerate(((0, 1), (1, 3))):
                    ins = dve.tensor_reduce(negmax[:, 2 * n + t:2 * n + t + 1], probs[:, n, lo:hi].rearrange("p b k -> p (b k)"),
                                            AX.X, ALU.max)
                link(ins)
                dve.tensor_scalar(negmax[:, 2 * n:2 * n + 2], negmax[:, 2 * n:2 * n + 2], -1.0, None, ALU.mult
                                  ).then_inc(sem("dsa_max"), 1)
            for hh in range(2):
                n = 2 * par + hh
                dve.wait_ge(sem("dsa_exp"), j * 2 + hh + 1)
                link(dve.reciprocal(prec[:, 2 * n:2 * n + 2], psums[:, 2 * n:2 * n + 2]))
                for t, (lo, hi) in enumerate(((0, 1), (1, 3))):
                    ins = dve.tensor_scalar(probs[:, n, lo:hi], probs[:, n, lo:hi], prec[:, 2 * n + t:2 * n + t + 1], None,
                                            ALU.mult)
                ins.then_inc(sem("dsa_probs"), 1)

        def dsa_low(j):
            for hh in range(2):
                dve.wait_ge(sem("dsa_high"), j * 2 + hh + 1)
                o = bass.ds(j * 2 + hh, 1)
                dve.tensor_tensor(att_lo[:, o], bank[6 + hh][:, 0:T].unsqueeze(1), att_hi[:, o].bitcast(F32), ALU.subtract
                                  ).then_inc(sem("dsa_operand"), 1)

        def dsa_behind(s, c):
            if chunk_in(s - 3, FIRST_DQ, LAST_DQ):
                dsa_low(s - (FIRST_DQ + 3))
            if chunk_in(s - 1, FIRST_DQ, LAST_DQ):
                dsa_softmax(s - (FIRST_DQ + 1), 1 - c)

        def rope_queries(p, c):
            s = p * 2 + c
            dve.wait_ge(sem("swapped"), s + 1)
            tabs = (cos_i, sin_i) if isinstance(s, int) and s < FIRST_DQ else (cos_d, sin_d)
            rope(proj[c], 2, *tabs, qbuf[:, c], sem("roped"), bank_free[c])
            if isinstance(s, int) and 1 <= s <= FIRST_DQ:
                index_add(s - 1)
            if isinstance(s, int) and s == FIRST_DQ:
                select()
            dsa_behind(s, c)

        for p in range(4):
            if p == DQ:
                split_low(dve, p, 1)
                rope_queries(p, 0)
                rope_queries(p, 1)
            else:
                evacuating(dve, split_low, p, rope_queries)
        with link.loop(4, GB, DSA_PER) as p:
            evacuating(dve, split_low, p, rope_queries)

        def branch_b(i):
            def merge_b(p, c):
                multiplied(dve, p, c)
                dve.tensor_tensor(merged[:, bass.ds(i * 4 + 2 * c, 2)], proj[c], sg[:, c], ALU.mult).then_inc(bank_free[c], 1)
            evacuating(dve, split_low, i * 2 + GB + 1, merge_b)

        def attention_end(p, c):
            dsa_behind(2 * p + c, c)
            if c:
                dsa_low(7)

        evacuating(dve, split_low, GB, attention_end)

        dve.wait_ge(sem("gate_logits"), 1)
        for n in range(8):
            ins = dve.tensor_scalar(gz[:, n], bank[2 + n // 2][:, (n % 2) * T:(n % 2 + 1) * T],
                                    gains[:, G_BIAS + n:G_BIAS + n + 1], None, ALU.add)
        ins.then_inc(sem("gate_biased"), 1)
        branch_b(0)
        dve.wait_ge(sem("gate_biased"), 1)
        flat = "p n t -> p (n t)"
        dve.scalar_tensor_tensor(out=ge.rearrange(flat), in0=gz.rearrange(flat), scalar=-1.0, in1=gz.rearrange(flat),
                                 op0=ALU.mult, op1=ALU.max).then_inc(sem("gate_abs"), 1)
        evacuating(dve, split_low, GB + 2, nothing)
        branch_b(1)
        dve.wait_ge(sem("gate_ln"), 1)
        link(dve.scalar_tensor_tensor(out=gz.rearrange(flat), in0=gz.rearrange(flat), scalar=0.0, in1=ge.rearrange(flat),
                                      op0=ALU.min, op1=ALU.subtract))
        evacuating(dve, split_low, GB + 4, nothing)
        branch_b(2)
        for n in range(8):
            ins = dve.tensor_tensor_scan(cum[:, n], ones, gz[:, n], 0.0, ALU.mult, ALU.add)
        ins.then_inc(sem("gates_summed"), 1)
        dve.wait_ge(sem("gates_summed"), 1)
        evacuating(dve, split_low, GB + 6, nothing)
        branch_b(3)

        def gla_head(h):
            def level_diff(lev):
                m = P >> lev
                blocks = "p a (n m) -> p (a n) m"
                c = cum[:, bass.ds(h * 2, 2)].rearrange(blocks, m=2 * m)
                dve.tensor_tensor(decay[lev % 2].rearrange(blocks, m=2 * m), c, c[:, :, m - 1:m].broadcast_to([P, T // m, 2 * m]),
                                  ALU.subtract).then_inc(sem("gla_diff"), 1)

            def level_z(lev):
                m = P >> lev
                dve.wait_ge(sem("gla_decay"), h * 8 + lev + 1)
                wait(dve, sem("gla_scored"), h * 9 + lev - 2)
                for f, x in ((0, kg), (1, qg)):
                    z, x, e = (halves(y, m)[:, :, f] for y in (zlev[lev % 3], x, decay[lev % 2]))
                    ins = dve.tensor_tensor(z, x, e, ALU.mult)
                ins.then_inc(sem("gla_z"), 1)

            def levels_ahead(lo, hi):
                for lev in range(lo, hi):
                    level_diff(lev)
                    level_z(lev)

            def levels_added(lo, hi):
                for lev in range(lo, hi):
                    dve.wait_ge(sem("gla_scored"), h * 9 + lev + 1)
                    b = bank[2 + lev % 3]
                    if lev == 0:
                        dve.tensor_copy(attn[:, 1], b[:, 0:P]).then_inc(sem("gla_added"), 1)
                        continue
                    m = (mask(lev - 1) if lev < 8 else ident).unsqueeze(1).broadcast_to([P, 2, P])
                    src = b[:, 0:T].rearrange("p (b i) -> p b i", b=2)
                    if lev == 1:
                        dve.tensor_tensor(attn[:, 0:3:2], src, m, ALU.mult).then_inc(sem("gla_added"), 1)
                        continue
                    dve.tensor_tensor(masked, src, m, ALU.mult).then_inc(sem("gla_added"), 1)
                    dve.wait_ge(sem("gla_added"), h * 9 + lev + 1)
                    ins = dve.tensor_tensor(attn[:, 0:3:2], attn[:, 0:3:2], masked, ALU.add)
                    if lev == 8:
                        ins.then_inc(sem("gla_attn"), 1)
                    else:
                        link(ins)

            p = h * 3 + GL
            evacuating(dve, split_low, p, nothing)
            dve.wait_ge(bank_free[1], p + 1)
            levels_ahead(0, 3)
            split_low(dve, p + 1, 1)
            levels_added(0, 3)
            levels_ahead(3, 6)
            split_low(dve, p + 2, 0)
            levels_added(3, 6)
            levels_ahead(6, 8)
            split_low(dve, p + 2, 1)
            levels_added(6, 9)
            split_low(dve, p + 3, 0)
            dve.wait_ge(sem("gla_root"), h + 1)
            link(dve.reciprocal(rstd, rstd))
            for e in range(4):
                ins = dve.scalar_tensor_tensor(out=onorm[:, e], in0=bank[6 + e // 2][:, (e % 2) * T:(e % 2 + 1) * T],
                                               scalar=gains[:, bass.ds(h * 4 + G_HEAD + e, 1)], in1=rstd, op0=ALU.mult,
                                               op1=ALU.mult)
            link(ins)
            dve.wait_ge(bank_free[1], p + 3)
            dve.tensor_tensor(onorm, onorm, swish, ALU.mult).then_inc(sem("gla_gated"), 1)
            dve.wait_ge(sem("gla_high"), h + 1)
            o = bass.ds(h * 4, 4)
            dve.tensor_tensor(att_lo[:, o], onorm, att_hi[:, o].bitcast(F32), ALU.subtract).then_inc(sem("gla_operand"), 1)

        gla_head(0)
        with link.loop(1, GLA_H, GLA_PER) as h:
            gla_head(h)

        def merge_a(i):
            def evac(p, c):
                multiplied(dve, p, c)
                link(dve.tensor_tensor(sg[:, c], proj[c], sg[:, c], ALU.mult))
                m = merged[:, bass.ds(i * 4 + 2 * c, 2)]
                dve.tensor_tensor(m, m, sg[:, c], ALU.add).then_inc(bank_free[c], 1)
            return evac

        def branch_a(i):
            evacuating(dve, split_low, i * 2 + GA + 1, merge_a(i))

        for i in range(3):
            evacuating(dve, split_low, i * 2 + GA, nothing)
            branch_a(i)
        sum_tiles(dve, "mem")
        evacuating(dve, split_low, GA + 6, nothing)
        norm_scale(dve, link, "mem", memT, G_MEM, range(2))
        split_low(dve, GA + 7, 1)
        norm_scale(dve, link, "mem", memT, G_MEM, range(2, 4))
        operand_low(dve, "mem", scr, act_hi, act_lo)
        merge_a(3)(GA + 7, 0)
        split_low(dve, XK, 0)
        merge_a(3)(GA + 7, 1)
        operand_low(dve, "merged", merged, att_hi, att_lo)

        def run(first, lo, hi, evac=None):
            def step(i):
                def add_residual(p, c):
                    multiplied(dve, p, c)
                    r = hT[:, bass.ds(i * 4 + 2 * c, 2)]
                    dve.tensor_tensor(r, r, proj[c], ALU.add).then_inc(bank_free[c], 1)
                evacuating(dve, split_low, i + first, evac or add_residual)
            over(dve, lo, hi, step)

        run(XK, 0, 4, nothing)
        run(WO, 0, 4)
        run(XV, 0, 1, nothing)
        sum_tiles(dve, "h2")
        run(XV, 1, 2, nothing)
        norm_scale(dve, link, "h2", hT, G_X, range(2))
        split_low(dve, XV + 2, 1)
        norm_scale(dve, link, "h2", hT, G_X, range(2, 4))
        split_low(dve, XV + 3, 0)
        run(XV, 3, 4, nothing)

        def cross_max(h):
            dve.wait_ge(sem("cross_scored"), h + 1)
            m = negmax[:, 2 * (h % 2):2 * (h % 2) + 2]
            link(dve.tensor_reduce(m, bank[2 + h % 2].rearrange("p (t m) -> p t m", t=TT), AX.X, ALU.max))
            dve.tensor_scalar(m, m, -(XD ** -0.5), None, ALU.mult).then_inc(sem("cross_max"), 1)

        def cross_probs(h):
            n = 2 * (h % 2)
            dve.wait_ge(sem("cross_exp"), h + 1)
            link(dve.reciprocal(prec[:, n:n + 2], psums[:, n:n + 2]))
            for t in range(TT):
                ins = dve.tensor_scalar(px[:, h % 2, t], px[:, h % 2, t], prec[:, n + t:n + t + 1], None, ALU.mult)
            ins.then_inc(sem("cross_probs"), 1)

        def cross_low(h):
            dve.wait_ge(sem("cross_high"), h + 1)
            for n in range(2):
                o = slice(4 * h + 2 * n, 4 * h + 2 * n + 2)
                ins = dve.tensor_tensor(act_lo[:, o], bank[6 + n].rearrange("p (e t) -> p e t", e=2), act_hi[:, o].bitcast(F32),
                                        ALU.subtract)
            ins.then_inc(sem("cross_operand"), 1)

        for h in range(XH):
            def attend(p, c, h=h):
                if c == 0 and h >= 2:
                    cross_low(h - 2)
                if c == 0 and h >= 1:
                    cross_max(h - 1)
                    cross_probs(h - 1)
            evacuating(dve, split_low, XQ + h, attend)
        cross_max(XH - 1)
        cross_low(XH - 2)
        cross_probs(XH - 1)
        cross_low(XH - 1)

        run(XO, 0, 4)
        dve.wait_ge(bank_free[1], PQ)
        squares(dve, "h3", hT, (1, 3), on_activation=False)
        sum_tiles(dve, "h3")
        norm_scale(dve, link, "h3", hT, G_FFN, range(2))
        for q in (2, 3):
            operand_low(dve, "h3", scr, att_hi, att_lo, quarters=(q - 2,))
            norm_scale(dve, link, "h3", hT, G_FFN, (q,))
        operand_low(dve, "h3", scr, att_hi, att_lo, quarters=(2, 3))

        def norm_rows(t):
            if t == 0:
                dve.wait_ge(sem("row_root"), 1)
                link(dve.reciprocal(stat[:, 2:4], stat[:, 0:2]))
                dve.wait_ge(sem("ffn_gain_landed"), 16 * TT)
            link(dve.scalar_tensor_tensor(out=xnN[:, t], in0=hN[:, t], scalar=stat[:, 2 + t:3 + t], in1=xnN[:, t], op0=ALU.mult,
                                          op1=ALU.mult))

        def top16(*rows):
            link(*[dve.max(v[:, 0:8], src) for v, i, src, rest in rows])
            link(*[dve.max_index(i[:, 0:8], v[:, 0:8], src) for v, i, src, rest in rows],
                 *[dve.match_replace(rest, v[:, 0:8], src, TAKEN) for v, i, src, rest in rows])
            link(*[dve.max(v[:, 8:16], rest) for v, i, src, rest in rows])
            link(*[dve.max_index(i[:, 8:16], v[:, 8:16], rest) for v, i, src, rest in rows])

        wide = [P, PTOP, PTOP]
        iota = consts[:, C_IOTA:C_IOTA + PTOP].unsqueeze(1).broadcast_to(wide)

        def route(g):
            at = bass.ds(g * PTOP, PTOP)
            link(dve.tensor_copy(sc, sims[:, bass.ds(g, 1)].rearrange("p g s n -> p (g s) n")))
            top16(*[(tv[:, s], ti[:, s], sc[:, s], sc2[:, s]) for s in range(2)])
            wait(dve, sem("gate_exped"), g)
            link(dve.tensor_copy(tif, ti),
                 dve.tensor_tensor(cand, tv[:, 0].unsqueeze(2).broadcast_to(wide), tv[:, 1].unsqueeze(1).broadcast_to(wide),
                                   ALU.add))
            top16((cv, ci, cand.rearrange("p a b -> p (a b)"), cand2.rearrange("p a b -> p (a b)")))
            dve.tensor_scalar(stat[:, 4:5], cv[:, 0:1], -1.0, None, ALU.mult).then_inc(sem("cands_ready"), 1)
            link(dve.tensor_scalar(cpart[:, 0], ci, 4, None, ALU.logical_shift_right),
                 dve.tensor_scalar(cpart[:, 1], ci, PTOP - 1, None, ALU.bitwise_and))
            link(dve.tensor_copy(cpartf, cpart))
            hot = (onehot, cand2)
            link(*[dve.tensor_tensor(hot[s], cpartf[:, s].unsqueeze(2).broadcast_to(wide), iota, ALU.is_equal)
                   for s in range(2)])
            link(*[dve.tensor_tensor(hot[s], hot[s], tif[:, s].unsqueeze(1).broadcast_to(wide), ALU.mult) for s in range(2)])
            link(*[dve.tensor_reduce(isel_all[:, s, at], hot[s], AX.X, ALU.add) for s in range(2)])
            dve.scalar_tensor_tensor(out=idx_all[:, at], in0=isel_all[:, 0, at], scalar=float(NKEYS), in1=isel_all[:, 1, at],
                                     op0=ALU.mult, op1=ALU.add).then_inc(sem("routed"), 1)
            dve.wait_ge(sem("gate_exped"), g + 1)
            link(dve.reciprocal(stat[:, 5:6], stat[:, 5:6]))
            link(dve.tensor_scalar(gates_all[:, at], egate, stat[:, 5:6], None, ALU.mult))

        def dot_rows(g, t):
            for k in range(PTOP):
                dve.wait_ge(u_landed[k % RING], g * 32 + (k // RING + 1) * 16)
                u = row_tile(k, first=isinstance(g, int) and g == 0)
                dve.tensor_tensor_reduce(u, u, xnN[:, t], 1.0, 0.0, ALU.mult, ALU.add, dots[:, k:k + 1]
                                         ).then_inc(sem("dotted"), 1)

        def weigh(g):
            at = bass.ds(g * PTOP, PTOP)
            dve.wait_ge(sem("gelu_ready"), g + 1)
            dve.tensor_tensor(w_all[:, at], gelu, gates_all[:, at], ALU.mult).then_inc(sem("weights_ready"), 1)

        def mark_rows(c):
            if isinstance(c, int):
                dve.wait_ge(sem("tables_turned"), c // PEER_H + 1)
            for k in range(SPREAD):
                if k == PLACES:
                    dve.wait_ge(sem("token_spread"), c * SPREAD)
                    for j in range(PLACES, SPREAD, 4):
                        dve.tensor_tensor(col_hot[:, j:j + 4], consts[:, C_IOTA:].unsqueeze(1).broadcast_to([P, 4, NKEYS]),
                                          turned[:, 1, bass.ds(c * SPREAD + j, 4)].unsqueeze(2).broadcast_to([P, 4, NKEYS]),
                                          ALU.is_equal).then_inc(sem("more_places"), 1)
                dve.wait_ge(sem("token_spread"), c * SPREAD + (k + 1 - RING))
                token = bass.ds(c * SPREAD + k, 1)
                dve.tensor_scalar(row_hot[:, k % RING], consts[:, C_IOTA:], turned[:, 0, token], turned[:, 2, token],
                                  ALU.is_equal, ALU.mult).then_inc(sem("rows_ready"), 1)

        def values_low(at, steps, first=False):
            for n in steps:
                dve.wait_ge(sem("v_high"), at * 4 + n + 1)
                if not (first and n < 2):
                    dve.wait_ge(sem("v_used"), at * 4 + (n - 1))
                dve.tensor_tensor(v_lo[:, n % 2], v_raw[n % 4], v_hi[:, n % 2].bitcast(F32), ALU.subtract
                                  ).then_inc(sem("v_split"), 1)

        def late_rows(g, phase):
            with dve.Fori(0, 4) as i:
                for k in range(4):
                    at = i * 3 + (LATE_UNIT // 4 + 12 * phase)
                    values_low(at, (3 * k,))
                    dve.wait_ge(sem(f"late_landed{k % 2}"), i * 32 + (phase * 128 + k // 2 * 16 + 16))
                    row = late_row[k % 2]
                    if phase % 2 == 0:
                        dve.tensor_tensor_reduce(row, row, xnN[:, 1], 1.0, 0.0, ALU.mult, ALU.add, late_dots[:, k:k + 1]
                                                 ).then_inc(sem("late_used"), 1)
                    else:
                        dve.wait_ge(sem("late_used"), i * 4 + (phase * PTOP + k))
                        dve.scalar_tensor_tensor(out=late_sum, in0=row, scalar=w_all[:, bass.ds(i * 4 + (g * PTOP + k), 1)],
                                                 in1=late_sum, op0=ALU.mult, op1=ALU.add).then_inc(sem("late_used"), 1)
                    values_low(at, (3 * k + 1, 3 * k + 2))
                    if phase % 2 == 0 and k == 3:
                        dve.wait_ge(sem("late_used"), i * 4 + (phase * PTOP + 4))
                        dve.tensor_copy(dots[:, bass.ds(i * 4, 4)], late_dots).then_inc(sem("late_dots"), 1)
                        dve.wait_ge(sem("late_dots"), i + (2 * phase + 1))

        run(PQ, 0, 1, nothing)
        norm_rows(0)
        run(PQ, 1, 2, nothing)
        dve.wait_ge(sem("sims_ready"), 1)
        route(0)
        split_low(dve, PQ + 2, 1)
        norm_rows(1)
        split_low(dve, PQ + 3, 0)
        dve.wait_ge(sem("sims_ready"), 2)
        route(1)
        evacuating(dve, split_low, PQ + 3, nothing, last=True)
        dot_rows(0, 0)
        link(dve.memset(w_all[:, EARLY * PTOP:], 0.0))
        dve.wait_ge(sem("sims_ready"), PEER_H)
        route(2)
        weigh(0)
        route(3)
        with link.loop(1, 8, ROUTE_PER) as g:
            dot_rows(g, 0)
            route(g + 3)
            weigh(g)
        with link.loop(8, EARLY - 1, ROUTE_PER) as g:
            dot_rows(g, 1)
            route(g + 3)
            weigh(g)
        dot_rows(EARLY - 1, 1)
        weigh(EARLY - 1)
        for c in range(ALONE, PEER_H + 1):
            mark_rows(c)
        with dve.Fori(9, GROUPS) as c:
            mark_rows(c)
        values_low(0, range(2), first=True)
        dve.wait_ge(sem("first_high"), 1)
        hi, lo = (x[:, 0].rearrange("p i (a t) -> p i a t", a=TT) for x in (e_hi, e_lo))
        dve.tensor_tensor(lo, spread[:, :, 0:BATCH].rearrange("p a i t -> p i a t"), hi.bitcast(F32), ALU.subtract
                          ).then_inc(sem("first_split"), 1)
        values_low(0, range(2, 16), first=True)
        values_low(4, range(16))
        for n, g in enumerate(LATE):
            late_rows(g, 2 * n)
            if n == 0:
                dve.wait_ge(sem("e_split"), 7)
                link(dve.memset(late_sum, 0.0))
            weigh(g)
            dve.wait_ge(sem("weights_ready"), g + 1)
            late_rows(g, 2 * n + 1)
        with dve.Fori(14, 16) as b:
            values_low(b * 4, range(16))

        dve.wait_ge(sem("v_used"), 2 * NKEYS)
        link(dve.tensor_copy(hN[:, 1, 3 * 512:], bank[7]))
        link(dve.tensor_tensor_reduce(hN[:, 1, 3 * 512:], hN[:, 1, 3 * 512:], hN[:, 1, 3 * 512:], 1.0, 0.0, ALU.mult, ALU.add,
                                      gsum[:, 7:8]))
        dve.wait_ge(sem("out_squares"), 1)
        dve.tensor_reduce(stat[:, 6:8], gsum.rearrange("p (t n) -> p t n", t=TT), AX.X, ALU.add).then_inc(sem("out_summed"), 1)
        dve.wait_ge(sem("out_root"), 1)
        link(dve.reciprocal(stat[:, 0:2], stat[:, 6:8]))
        dve.wait_ge(sem("final_gain_landed"), 16)
        for t in range(TT):
            for n in range(4):
                c = slice(n * 512, (n + 1) * 512)
                dve.scalar_tensor_tensor(out=hN[:, t, c], in0=bank[4 * t + n], scalar=stat[:, t:t + 1], in1=gfin[:, c],
                                         op0=ALU.mult, op1=ALU.mult).then_inc(sem("out_ready"), 1)

    ctx.close()


DSA_PER = 14
GLA_PER = 8
ROUTE_PER = 29

_INS = ['x', 'mem', 'positions', 'norm_mix_g', 'w_in', 'gla_gate_w2', 'gla_gate_b', 'gla_head_norm_g', 'w_proj_gla',
        'w_proj_dsa', 'w_out', 'norm_x_g', 'norm_mem_g', 'w_xq', 'w_xk', 'w_xv', 'w_xo', 'norm_ffn_g', 'peer_wq',
        'peer_sub_keys', 'peer_u', 'peer_v', 'norm_final_g']


def kernel(**inputs):
    import concourse.bacc as bacc
    from concourse.bass_utils import run_bass_kernel_spmd

    nc = bacc.Bacc("TRN2", target_bir_lowering=False, num_devices=1)
    arrays = {f"in_{n}": np.ascontiguousarray(inputs[n]) for n in _INS}
    arrays["in_consts"] = constants()
    args = {n[3:]: nc.dram_tensor(n, v.shape, mybir.dt.from_np(v.dtype), kind="ExternalInput").ap() for n, v in arrays.items()}
    args["out"] = nc.dram_tensor("out_0", (1, T, D), F32, kind="ExternalOutput").ap()
    hybrid_block(nc, args)
    r = run_bass_kernel_spmd(nc, [arrays], core_ids=[0])
    return r.results[0]["out_0"]
```
